# Optimizing a Trainium2 kernel written in Bass

```python
import math
import jax, jax.numpy as jnp
from jax import lax
import numpy as np

D_MODEL = 1024
BATCH = 1
SEQ = 512
DEPTH = 1

N_META = 16
BLOCK = 128
ROPE_THETA = 10000.0
EPS = 1e-6

A_HEADS = 4
A_HEAD_DIM = 64
A_V_DIM = 2 * A_HEAD_DIM
A_QK_WIDTH = A_HEADS * 2 * A_HEAD_DIM
A_OUT = A_HEADS * A_V_DIM

B_HEADS = 8
B_HEAD_DIM = 64
B_OUT = B_HEADS * B_HEAD_DIM
IDX_HEADS = 8
IDX_DIM = 64
IDX_ROPE_DIM = 32
TOPK_CAP = 256

PEER_HEADS = 8
N_KEYS = 128
N_EXPERTS = N_KEYS * N_KEYS
PEER_KEY_DIM = 128
PEER_HALF = PEER_KEY_DIM // 2
PEER_TOPK = 16

SPLIT_SIZES = (
    A_QK_WIDTH, A_QK_WIDTH, A_OUT,
    B_OUT, B_HEAD_DIM, B_HEAD_DIM,
    IDX_HEADS * IDX_DIM, IDX_DIM, IDX_HEADS,
    D_MODEL, D_MODEL,
)
IN_WIDTH = int(sum(SPLIT_SIZES))
SPLIT_POINTS = tuple(int(v) for v in np.cumsum(SPLIT_SIZES)[:-1])

kernel_name = "hybrid_diffattn_dsa_peer_block"

def rms_norm(x, gain):
    xf = x.astype(jnp.float32)
    y = xf * lax.rsqrt(jnp.mean(xf * xf, axis=-1, keepdims=True) + EPS)
    return (y * gain.astype(jnp.float32)).astype(x.dtype)

def rope_tables(t_len, dim):
    inv = ROPE_THETA ** (-jnp.arange(0, dim, 2, dtype=jnp.float32) / dim)
    ang = jnp.arange(t_len, dtype=jnp.float32)[:, None] * inv[None, :]
    return jnp.cos(ang), jnp.sin(ang)

def apply_rope(x, cos, sin):
    half = x.shape[-1] // 2
    x1, x2 = x[..., :half], x[..., half:]
    c = cos[None, :, None, :].astype(x.dtype)
    s = sin[None, :, None, :].astype(x.dtype)
    return jnp.concatenate([x1 * c - x2 * s, x2 * c + x1 * s], axis=-1)

def masked_softmax(scores, mask):
    s = jnp.where(mask, scores.astype(jnp.float32), -jnp.inf)
    return jax.nn.softmax(s, axis=-1)

def diff_attention(q1, q2, k1, k2, v, lam):
    bsz, t_len, n_h, dv = v.shape
    n_blocks = t_len // BLOCK
    scale = A_HEAD_DIM ** -0.5
    key_pos = jnp.arange(t_len)

    def one_block(i):
        start = i * BLOCK
        qb1 = lax.dynamic_slice_in_dim(q1, start, BLOCK, axis=1)
        qb2 = lax.dynamic_slice_in_dim(q2, start, BLOCK, axis=1)
        causal = key_pos[None, :] <= (start + jnp.arange(BLOCK))[:, None]
        p1 = masked_softmax(jnp.einsum('bqhd,bkhd->bhqk', qb1, k1) * scale, causal)
        p2 = masked_softmax(jnp.einsum('bqhd,bkhd->bhqk', qb2, k2) * scale, causal)
        return jnp.einsum('bhqk,bkhd->bqhd', (p1 - lam * p2).astype(v.dtype), v)

    out = lax.map(one_block, jnp.arange(n_blocks))
    return out.transpose(1, 0, 2, 3, 4).reshape(bsz, t_len, n_h, dv)

def dsa_attention(q, k, v, iq, ik, iw, k_sel):
    bsz, t_len, n_h, d = q.shape
    n_blocks = t_len // BLOCK
    scale = B_HEAD_DIM ** -0.5
    key_pos = jnp.arange(t_len)

    def one_block(i):
        start = i * BLOCK
        qpos = start + jnp.arange(BLOCK)
        qb = lax.dynamic_slice_in_dim(q, start, BLOCK, axis=1)
        iqb = lax.dynamic_slice_in_dim(iq, start, BLOCK, axis=1)
        iwb = lax.dynamic_slice_in_dim(iw, start, BLOCK, axis=1)
        causal = key_pos[None, :] <= qpos[:, None]
        logits = jax.nn.relu(jnp.einsum('bqhd,bkd->bqhk', iqb, ik))
        index_score = jnp.einsum('bqh,bqhk->bqk', iwb, logits)
        index_score = jnp.where(causal[None], index_score.astype(jnp.float32), -jnp.inf)
        _, top_idx = lax.top_k(index_score, k_sel)
        valid = top_idx <= qpos[None, :, None]
        flat = top_idx.reshape(bsz, BLOCK * k_sel)[..., None]
        ks = jnp.take_along_axis(k, flat, axis=1).reshape(bsz, BLOCK, k_sel, d)
        vs = jnp.take_along_axis(v, flat, axis=1).reshape(bsz, BLOCK, k_sel, d)
        p = masked_softmax(jnp.einsum('bqhd,bqkd->bqhk', qb, ks) * scale, valid[:, :, None, :])
        return jnp.einsum('bqhk,bqkd->bqhd', p.astype(v.dtype), vs)

    out = lax.map(one_block, jnp.arange(n_blocks))
    return out.transpose(1, 0, 2, 3, 4).reshape(bsz, t_len, n_h, d)

def peer_ffn(xn, w_query, sub_keys, u, v):
    n_tok, d_model = xn.shape

    def one_block(xb):
        q = (xb @ w_query).reshape(BLOCK, PEER_HEADS, 2, PEER_HALF)
        s = jnp.einsum('thcd,hckd->thck', q, sub_keys)
        s1, i1 = lax.top_k(s[:, :, 0], PEER_TOPK)
        s2, i2 = lax.top_k(s[:, :, 1], PEER_TOPK)
        cand_s = (s1[..., :, None] + s2[..., None, :]).reshape(BLOCK, PEER_HEADS, PEER_TOPK * PEER_TOPK)
        cand_i = (i1[..., :, None] * N_KEYS + i2[..., None, :]).reshape(BLOCK, PEER_HEADS, PEER_TOPK * PEER_TOPK)
        top_s, top_c = lax.top_k(cand_s, PEER_TOPK)
        expert = jnp.take_along_axis(cand_i, top_c, axis=-1)
        g = jax.nn.softmax(top_s.astype(jnp.float32), axis=-1).astype(xb.dtype)
        ue = jnp.take(u, expert, axis=0)
        ve = jnp.take(v, expert, axis=0)
        act = jax.nn.gelu(jnp.einsum('thkd,td->thk', ue, xb), approximate=False)
        return jnp.einsum('thk,thkd->td', g * act, ve)

    out = lax.map(one_block, xn.reshape(n_tok // BLOCK, BLOCK, d_model))
    return out.reshape(n_tok, d_model)

def setup_inputs(seed: int = 0) -> dict:
    key = jax.random.key(seed)
    ks = jax.random.split(key, 24)
    f32 = jnp.float32

    def nrm(k, shape, scale):
        return jax.random.normal(k, shape, f32) * scale

    def gain(k, shape):
        return 1.0 + 0.02 * jax.random.normal(k, shape, f32)

    return {
        "x": nrm(ks[0], (BATCH, SEQ, D_MODEL), 1.0),
        "meta_tokens": nrm(ks[1], (N_META, D_MODEL), 1.0),
        "mix_norm_gain": gain(ks[2], (DEPTH, D_MODEL)),
        "w_in": nrm(ks[3], (DEPTH, D_MODEL, IN_WIDTH), D_MODEL ** -0.5),
        "a_q_norm_gain": gain(ks[4], (DEPTH, A_HEAD_DIM)),
        "a_k_norm_gain": gain(ks[5], (DEPTH, A_HEAD_DIM)),
        "a_lambda_q1": nrm(ks[6], (DEPTH, A_HEAD_DIM), 0.1),
        "a_lambda_k1": nrm(ks[7], (DEPTH, A_HEAD_DIM), 0.1),
        "a_lambda_q2": nrm(ks[8], (DEPTH, A_HEAD_DIM), 0.1),
        "a_lambda_k2": nrm(ks[9], (DEPTH, A_HEAD_DIM), 0.1),
        "a_subln_gain": gain(ks[10], (DEPTH, A_V_DIM)),
        "w_branch_a": nrm(ks[11], (DEPTH, A_OUT, D_MODEL), A_OUT ** -0.5),
        "b_q_norm_gain": gain(ks[12], (DEPTH, B_HEAD_DIM)),
        "b_k_norm_gain": gain(ks[13], (DEPTH, B_HEAD_DIM)),
        "w_branch_b": nrm(ks[14], (DEPTH, B_OUT, D_MODEL), B_OUT ** -0.5),
        "w_out": nrm(ks[15], (DEPTH, D_MODEL, D_MODEL), D_MODEL ** -0.5),
        "ffn_norm_gain": gain(ks[16], (DEPTH, D_MODEL)),
        "peer_w_query": nrm(ks[17], (DEPTH, D_MODEL, PEER_HEADS * PEER_KEY_DIM), D_MODEL ** -0.5),
        "peer_sub_keys": nrm(ks[18], (DEPTH, PEER_HEADS, 2, N_KEYS, PEER_HALF), PEER_HALF ** -0.5),
        "peer_u": nrm(ks[19], (DEPTH, N_EXPERTS, D_MODEL), D_MODEL ** -0.5),
        "peer_v": nrm(ks[20], (DEPTH, N_EXPERTS, D_MODEL), (PEER_HEADS * PEER_TOPK) ** -0.5),
    }

def reference(x, meta_tokens, mix_norm_gain, w_in, a_q_norm_gain, a_k_norm_gain,
              a_lambda_q1, a_lambda_k1, a_lambda_q2, a_lambda_k2, a_subln_gain, w_branch_a,
              b_q_norm_gain, b_k_norm_gain, w_branch_b, w_out, ffn_norm_gain,
              peer_w_query, peer_sub_keys, peer_u, peer_v):
    bsz, seq, d_model = x.shape
    t_real = N_META + seq
    t_pad = ((t_real + BLOCK - 1) // BLOCK) * BLOCK
    k_sel = min(TOPK_CAP, seq // 4)

    meta = jnp.broadcast_to(meta_tokens.astype(x.dtype)[None], (bsz, N_META, d_model))
    pad = jnp.zeros((bsz, t_pad - t_real, d_model), x.dtype)
    h = jnp.concatenate([meta, x, pad], axis=1)

    cos, sin = rope_tables(t_pad, A_HEAD_DIM)
    icos, isin = rope_tables(t_pad, IDX_ROPE_DIM)

    for layer in range(DEPTH):
        lambda_init = 0.8 - 0.6 * math.exp(-0.3 * layer)
        xn = rms_norm(h, mix_norm_gain[layer])
        proj = xn @ w_in[layer]
        aq, ak, av, bq, bk, bv, iq, ik, iw, gate_a, gate_b = jnp.split(proj, SPLIT_POINTS, axis=-1)

        aq = apply_rope(rms_norm(aq.reshape(bsz, t_pad, 2 * A_HEADS, A_HEAD_DIM), a_q_norm_gain[layer]), cos, sin)
        ak = apply_rope(rms_norm(ak.reshape(bsz, t_pad, 2 * A_HEADS, A_HEAD_DIM), a_k_norm_gain[layer]), cos, sin)
        aq = aq.reshape(bsz, t_pad, A_HEADS, 2, A_HEAD_DIM)
        ak = ak.reshape(bsz, t_pad, A_HEADS, 2, A_HEAD_DIM)
        av = av.reshape(bsz, t_pad, A_HEADS, A_V_DIM)
        lam = (jnp.exp(jnp.sum(a_lambda_q1[layer].astype(jnp.float32) * a_lambda_k1[layer].astype(jnp.float32)))
               - jnp.exp(jnp.sum(a_lambda_q2[layer].astype(jnp.float32) * a_lambda_k2[layer].astype(jnp.float32)))
               + lambda_init)
        a_out = diff_attention(aq[..., 0, :], aq[..., 1, :], ak[..., 0, :], ak[..., 1, :], av, lam)
        a_out = rms_norm(a_out, a_subln_gain[layer]) * (1.0 - lambda_init)
        y_a = a_out.reshape(bsz, t_pad, A_OUT) @ w_branch_a[layer]

        bq = apply_rope(rms_norm(bq.reshape(bsz, t_pad, B_HEADS, B_HEAD_DIM), b_q_norm_gain[layer]), cos, sin)
        bk = apply_rope(rms_norm(bk.reshape(bsz, t_pad, 1, B_HEAD_DIM), b_k_norm_gain[layer]), cos, sin)[:, :, 0]
        iq = iq.reshape(bsz, t_pad, IDX_HEADS, IDX_DIM)
        iq = jnp.concatenate([apply_rope(iq[..., :IDX_ROPE_DIM], icos, isin), iq[..., IDX_ROPE_DIM:]], axis=-1)
        ik = ik[:, :, None, :]
        ik = jnp.concatenate([apply_rope(ik[..., :IDX_ROPE_DIM], icos, isin), ik[..., IDX_ROPE_DIM:]], axis=-1)[:, :, 0]
        iw = iw * (IDX_HEADS ** -0.5 * IDX_DIM ** -0.5)
        b_out = dsa_attention(bq, bk, bv, iq, ik, iw, k_sel)
        y_b = b_out.reshape(bsz, t_pad, B_OUT) @ w_branch_b[layer]

        mixed = jax.nn.sigmoid(gate_a) * y_a + jax.nn.sigmoid(gate_b) * y_b
        h = h + mixed @ w_out[layer]

        hn = rms_norm(h, ffn_norm_gain[layer]).reshape(bsz * t_pad, d_model)
        h = h + peer_ffn(hn, peer_w_query[layer], peer_sub_keys[layer], peer_u[layer], peer_v[layer]).reshape(bsz, t_pad, d_model)

    return h[:, N_META:N_META + seq]


_drawn_inputs = setup_inputs


def setup_inputs(seed=0):
    import zlib

    import numpy as np

    out = dict(_drawn_inputs(seed))
    spreads = {}
    factors = {'mix_norm_gain': 3.172,
     'a_q_norm_gain': 6.84,
     'a_k_norm_gain': 5.882,
     'a_lambda_q1': 5.029,
     'a_lambda_k2': 8.0,
     'a_subln_gain': 5.698,
     'b_q_norm_gain': 8.0,
     'b_k_norm_gain': 8.0,
     'ffn_norm_gain': 22.271}
    for name, (base, spread) in spreads.items():
        noise = np.random.default_rng([zlib.crc32(name.encode()), seed]).standard_normal(out[name].shape)
        drawn = base * np.exp(spread * noise) if base else spread * noise
        out[name] = __import__('jax').numpy.asarray(drawn.astype(out[name].dtype))
    for name, factor in factors.items():
        out[name] = (out[name] * factor).astype(out[name].dtype)
    return out
```

```python
import concourse.bass as bass
from concourse import mybir

F32 = mybir.dt.float32
F32R = mybir.dt.float32r
BF16 = mybir.dt.bfloat16
I32 = mybir.dt.int32
U32 = mybir.dt.uint32
ALU = mybir.AluOpType
ACT = mybir.ActivationFunctionType
X = mybir.AxisListType.X

P = 128
D = 1024
DC = D // P
SEQ = 512
NT = SEQ // P
META = 16
KEYS = META + SEQ
EPS = 1e-6

HEAD = 64
WIDE = 512
GROUPS = WIDE // HEAD
SMALL = 3 * HEAD + 8
A_HEADS = 4
B_HEADS = 8
IDX_HEADS = 8
IDX_ROPE = 32
TOPK = SEQ // 4
LAMBDA_INIT = 0.2

PEER_HEADS = 8
PEER_TOPK = 16
N_KEYS = 128
PICKS = PEER_HEADS * PEER_TOPK
ROWS = [(a, PEER_TOPK // (a + 1)) for a in range(PEER_TOPK)]
CANDS = sum(n for _, n in ROWS)

MASKED = -1e30
UNSEEN = -1e38
TAKEN = -3e38

CHUNKS = ["ak", "small", "av", "aq", "iq", "bq", "gate", "gate", "gate", "gate"]
WITH_META = ("ak", "small", "av")
ROTATED = ("ak", "small", "aq", "iq", "bq")
STEPS = [(c, kind, i) for c, kind in enumerate(CHUNKS)
         for i in range(NT + (kind in WITH_META))]
ROT_STEPS = [n for n, (_, kind, _) in enumerate(STEPS) if kind in ROTATED]

KB = 1024
BASE = 16896


def rows_of(i):
    return META if i == NT else P


def bcast(ap, axis, n):
    shape = list(ap.shape)
    shape.insert(axis, n)
    return ap.unsqueeze(axis).to_broadcast(shape)


class Layer:
    pass


def place_shared(nc, m):
    at = [BASE]

    def sb(name, shape, dt=F32):
        size = mybir.dt.size(dt)
        for n in shape[1:]:
            size *= n
        t = nc.alloc_sbuf_tensor_at(name, shape, dt, offset=at[0])
        at[0] += -(-size // 32) * 32
        return t

    m.stream = sb("stream", [P, NT, D])
    m.ident = sb("ident", [P, P])
    m.ident_b = sb("ident_b", [P, P], BF16)
    m.tri_b = sb("tri_b", [P, P], BF16)
    m.tri = sb("tri", [P, P])
    m.iota = sb("iota", [P, P])
    m.mix_gain = sb("mix_gain", [P, DC])
    m.ffn_gain = sb("ffn_gain", [P, DC])
    m.subln = sb("subln", [P, P])
    m.neg_lam = sb("neg_lam", [P, 1])
    m.iw = sb("iw", [P, NT, IDX_HEADS])
    m.free0 = at[0]
    m.xh = sb("xh", [P, DC, SEQ], F32R)
    m.xl = sb("xl", [P, DC, SEQ], F32R)
    m.free1 = at[0]
    m.aqT = sb("aqT", [P, 4, SEQ])
    m.bqT = sb("bqT", [P, 4, SEQ])
    m.iqT = sb("iqT", [P, 4, SEQ])
    m.akT = sb("akT", [P, 4, KEYS])
    m.bkT = sb("bkT", [P, KEYS])
    m.ikT = sb("ikT", [P, KEYS])
    m.av = sb("av", [P, NT + 1, WIDE])
    m.bv = sb("bv", [P, NT + 1, HEAD])
    m.gates = sb("gates", [P, NT, 2 * D])
    m.free2 = at[0]
    m.psum = nc.alloc_psum_tensor("psum", [P, 8 * 512], F32)


def bank(m, b, n=1):
    return m.psum[:, b * 512:(b + n) * 512]


def placer(nc, start, limit=16481 + 212860):
    at = [start]

    def sb(name, shape, dt=F32):
        size = mybir.dt.size(dt)
        for n in shape[1:]:
            size *= n
        size = -(-size // 32) * 32
        assert at[0] + size <= limit, (name, at[0] + size - limit)
        t = nc.alloc_sbuf_tensor_at(name, shape, dt, offset=at[0])
        at[0] += size
        return t
    return sb


def chain(engine, sem):
    n = [0]

    def link(ins):
        n[0] += 1
        ins.then_inc(sem, 1)
        engine.wait_ge(sem, n[0])
    return link


def inverse_root(nc, link, out, root, square):
    link(nc.vector.reciprocal(out, root))
    link(nc.vector.tensor_tensor(root, out, out, ALU.mult))
    link(nc.vector.tensor_tensor(root, root, square, ALU.mult))
    link(nc.vector.tensor_scalar(root, root, -0.5, 1.5, ALU.mult, ALU.add))
    link(nc.vector.tensor_tensor(out, out, root, ALU.mult))


def project(nc, m, d):
    wsb = placer(nc, m.free0)
    wch = wsb("wch", [P, 2, DC, WIDE])
    sb = placer(nc, m.free2)
    xT = sb("xT", [P, DC, KEYS])
    raw = sb("raw", [P, 2, WIDE])
    rot = sb("rot", [P, 2, WIDE])
    xn = sb("xn", [P, D])
    meta = sb("meta", [META, D])
    part = sb("part", [P, 2, WIDE])
    cos = sb("cos", [P, NT + 1, HEAD])
    sin = sb("sin", [P, NT + 1, HEAD])
    icos = sb("icos", [P, NT + 1, IDX_ROPE])
    isin = sb("isin", [P, NT + 1, IDX_ROPE])
    gained = {k: (sb("cos_" + k, [P, NT + 1, HEAD]), sb("sin_" + k, [P, NT + 1, HEAD]))
              for k in ("aq", "ak", "bq", "bk")}
    gains = sb("gains", [P, 4, HEAD])
    lams = sb("lams", [P, 4, HEAD])
    lamp = sb("lamp", [P, 2, HEAD])
    lam2 = sb("lam2", [P, 2])
    iota_i = sb("iota_i", [P, P], I32)
    sums = sb("sums", [P, 8])
    root = sb("root", [P, 8])
    inv = sb("inv", [P, 8])
    ms = sb("ms", [P, 8])

    x_loaded = [nc.alloc_semaphore(f"x_loaded{i}") for i in range(NT + 1)]
    consts = nc.alloc_semaphore("consts")
    w_loaded = [nc.alloc_semaphore(f"w_loaded{k}") for k in range(2)]
    pool_consts = nc.alloc_semaphore("pool_consts")
    squared = nc.alloc_semaphore("squared")
    ms_ready = nc.alloc_semaphore("ms_ready")
    root_ready = nc.alloc_semaphore("root_ready")
    lam_dots = nc.alloc_semaphore("lam_dots")
    lam_exps = nc.alloc_semaphore("lam_exps")
    xn_ready = nc.alloc_semaphore("xn_ready")
    xn_turned = nc.alloc_semaphore("xn_turned")
    xT_ready = nc.alloc_semaphore("xT_ready")
    projected = nc.alloc_semaphore("projected")
    evacuated = nc.alloc_semaphore("evacuated")
    head_ms = nc.alloc_semaphore("head_ms")
    head_root = nc.alloc_semaphore("head_root")
    rotated = nc.alloc_semaphore("rotated")
    turned = nc.alloc_semaphore("turned")
    turned_out = nc.alloc_semaphore("turned_out")
    dve_order = nc.alloc_semaphore("dve_order_a")
    pool_order = nc.alloc_semaphore("pool_order_a")
    N_CONSTS = 4 + 2 + 1 + 4 + 4

    with nc.Block() as block:
        @block.sync
        def _(sp):
            for i in range(NT):
                sp.dma_start(m.stream[:, i, :], d.x[i * P:(i + 1) * P, :]).then_inc(x_loaded[i], 16)
            sp.dma_start(meta[:], d.meta_tokens).then_inc(x_loaded[NT], 16)
            for c, kind in enumerate(CHUNKS):
                if c >= 2:
                    sp.wait_ge(projected, 1 + max(n for n, s in enumerate(STEPS) if s[0] == c - 2))
                if kind == "small":
                    sp.dma_start(wch[:, c % 2, :, 0:SMALL], d.w_small).then_inc(w_loaded[c % 2], 16)
                else:
                    w = c - (c > 1)
                    sp.dma_start(wch[:, c % 2], d.w_wide[w]).then_inc(w_loaded[c % 2], 16)

        @block.gpsimd
        def _(pool):
            link = chain(pool, pool_order)
            link(nc.gpsimd.memset(m.ident[:], 0.0))
            link(nc.gpsimd.memset(m.tri[:], 0.0))
            link(nc.gpsimd.affine_select(out=m.ident[:], in_=m.ident[:], compare_op=ALU.not_equal, fill=1.0,
                                         base=0, pattern=[[-1, P]], channel_multiplier=1))
            link(nc.gpsimd.affine_select(out=m.tri[:], in_=m.tri[:], compare_op=ALU.is_ge, fill=UNSEEN,
                                         base=0, pattern=[[-1, P]], channel_multiplier=1))
            nc.gpsimd.iota(iota_i[:], pattern=[[1, P]], base=0, channel_multiplier=0).then_inc(pool_consts, 1)

        @block.vector
        def _(dve):
            nc.vector.memset(sums[:], 1.0).then_inc(dve_order, 1)
            dve.wait_ge(pool_consts, 1)
            nc.vector.tensor_copy(m.ident_b[:], m.ident[:])
            nc.vector.tensor_scalar(m.tri_b[:], m.tri[:], MASKED / UNSEEN, None, ALU.mult)
            nc.vector.tensor_copy(m.iota[:], iota_i[:])
            dve.wait_ge(consts, 16 * N_CONSTS)
            h = HEAD // 2
            for g, (k, scale) in enumerate((("aq", HEAD ** -0.5), ("ak", 1.0), ("bq", HEAD ** -0.5), ("bk", 1.0))):
                cg, sg = gained[k]
                if g in (0, 2):
                    nc.vector.tensor_scalar(gains[:, g], gains[:, g], scale, None, ALU.mult).then_inc(dve_order, 1)
                    dve.wait_ge(dve_order, 2 + g // 2)
                nc.vector.tensor_tensor(cg[:], cos[:], bcast(gains[:, g], 1, NT + 1), ALU.mult)
                nc.vector.tensor_tensor(sg[:, :, 0:h], sin[:, :, 0:h], bcast(gains[:, g, h:], 1, NT + 1), ALU.mult)
                nc.vector.tensor_tensor(sg[:, :, h:], sin[:, :, h:], bcast(gains[:, g, 0:h], 1, NT + 1), ALU.mult)
            nc.vector.tensor_scalar(m.subln[:], m.subln[:], 1.0 - LAMBDA_INIT, None, ALU.mult)
            order = [3]

            def step(ins):
                order[0] += 1
                ins.then_inc(dve_order, 1)
                dve.wait_ge(dve_order, order[0])

            step(nc.vector.tensor_tensor(lamp[:], lams[:, 0:2], lams[:, 2:4], ALU.mult))
            nc.vector.tensor_reduce(lam2[:], lamp[:], X, ALU.add).then_inc(lam_dots, 1)
            dve.wait_ge(lam_exps, 1)
            step(nc.vector.tensor_tensor(m.neg_lam[:], lam2[:, 1:2], lam2[:, 0:1], ALU.subtract))
            step(nc.vector.tensor_scalar(m.neg_lam[:], m.neg_lam[:], -LAMBDA_INIT, None, ALU.add))

            dve.wait_ge(squared, NT + 1)
            nc.vector.tensor_scalar(ms[:, 0:NT + 1], sums[:, 0:NT + 1], 1.0 / D, EPS, ALU.mult, ALU.add).then_inc(ms_ready, 1)
            dve.wait_ge(root_ready, 1)
            inverse_root(nc, step, inv[:, 0:NT + 1], root[:, 0:NT + 1], ms[:, 0:NT + 1])
            for i in range(NT + 1):
                r = rows_of(i)
                src = m.stream[:, i, :] if i < NT else meta[:]
                if i >= 1:
                    dve.wait_ge(xn_turned, i)
                nc.vector.tensor_scalar(xn[0:r], src, inv[0:r, i:i + 1], None, ALU.mult).then_inc(xn_ready, 1)
                dve.wait_ge(xn_turned, i + 1)
                lo = META + i * P if i < NT else 0
                ps = bank(m, 6, 2).rearrange("p (c t) -> p c t", c=DC)[:, :, 0:r]
                nc.vector.tensor_tensor(xT[:, :, lo:lo + r], ps, bcast(m.mix_gain[:], 2, r),
                                        ALU.mult).then_inc(xT_ready, 1)

            def rotate(out, x, c, s, half):
                heads, r = x.shape[1], x.shape[0]
                a = part[0:r, 0, 0:heads * 2 * half].rearrange("p (h w) -> p h w", h=heads)
                b = part[0:r, 1, 0:heads * 2 * half].rearrange("p (h w) -> p h w", h=heads)
                nc.vector.tensor_tensor(a, x[:, :, 0:2 * half], bcast(c, 1, heads), ALU.mult)
                nc.vector.tensor_tensor(b[:, :, 0:half], x[:, :, half:2 * half], bcast(s[:, 0:half], 1, heads), ALU.mult)
                step(nc.vector.tensor_tensor(b[:, :, half:], x[:, :, 0:half], bcast(s[:, half:], 1, heads), ALU.mult))
                return nc.vector.tensor_tensor(out, a, b, ALU.add)

            def head_scale(x, heads, k):
                r = x.shape[0]
                sq = part[0:r, 0, 0:heads * HEAD].rearrange("p (h w) -> p h w", h=heads)
                step(nc.vector.tensor_tensor(sq, x, x, ALU.mult))
                step(nc.vector.tensor_reduce(ms[0:r, 0:heads], sq, X, ALU.add))
                nc.vector.tensor_scalar(ms[0:r, 0:heads], ms[0:r, 0:heads], 1.0 / HEAD, EPS,
                                        ALU.mult, ALU.add).then_inc(head_ms, 1)
                dve.wait_ge(head_root, k)
                inverse_root(nc, step, inv[0:r, 0:heads], root[0:r, 0:heads], ms[0:r, 0:heads])

            roots = 0
            for q, n in enumerate(ROT_STEPS):
                _, kind, i = STEPS[n]
                r = rows_of(i)
                dve.wait_ge(evacuated, n + 1)
                if q >= 1:
                    dve.wait_ge(rotated, q)
                if q >= 2:
                    dve.wait_ge(turned, q - 1)
                x = raw[0:r, q % 2]
                out = rot[0:r, q % 2]
                if kind == "small":
                    bk = x[:, 0:HEAD].rearrange("p (h w) -> p h w", h=1)
                    ik = x[:, 2 * HEAD:3 * HEAD].rearrange("p (h w) -> p h w", h=1)
                    o = out[:, 0:4 * HEAD].rearrange("p (h w) -> p h w", h=4)
                    roots += 1
                    head_scale(bk, 1, roots)
                    cg, sg = gained["bk"]
                    step(rotate(o[:, 0:1], bk, cg[0:r, i], sg[0:r, i], HEAD // 2))
                    step(nc.vector.tensor_scalar(o[:, 0], o[:, 0], inv[0:r, 0:1], None, ALU.mult))
                    step(rotate(o[:, 2:3, 0:IDX_ROPE], ik, icos[0:r, i], isin[0:r, i], IDX_ROPE // 2))
                    step(nc.vector.tensor_copy(o[:, 2, IDX_ROPE:], ik[:, 0, IDX_ROPE:]))
                    nc.vector.tensor_copy(m.bv[0:r, i], x[:, HEAD:2 * HEAD])
                    if i < NT:
                        nc.vector.tensor_scalar(m.iw[:, i], x[:, 3 * HEAD:SMALL], IDX_HEADS ** -0.5 * HEAD ** -0.5,
                                                None, ALU.mult)
                    nc.vector.tensor_copy(o[:, 1], o[:, 0])
                    nc.vector.tensor_copy(o[:, 3], o[:, 2]).then_inc(rotated, 1)
                    continue
                xh = x.rearrange("p (h w) -> p h w", h=GROUPS)
                oh = out.rearrange("p (h w) -> p h w", h=GROUPS)
                if kind == "iq":
                    nc.vector.tensor_copy(oh[:, :, IDX_ROPE:], xh[:, :, IDX_ROPE:])
                    rotate(oh[:, :, 0:IDX_ROPE], xh, icos[0:r, i], isin[0:r, i], IDX_ROPE // 2).then_inc(rotated, 1)
                    continue
                roots += 1
                head_scale(xh, GROUPS, roots)
                cg, sg = gained[kind]
                step(rotate(oh, xh, cg[0:r, i], sg[0:r, i], HEAD // 2))
                nc.vector.tensor_tensor(oh, oh, bcast(inv[0:r, 0:GROUPS], 2, HEAD), ALU.mult).then_inc(rotated, 1)

        @block.scalar
        def _(act):
            def bc(row):
                return row.partition_broadcast(P)
            act.dma_start(m.mix_gain[:], d.mix_gain).then_inc(consts, 16)
            act.dma_start(m.ffn_gain[:], d.ffn_gain).then_inc(consts, 16)
            for t, s in ((cos, d.cos), (sin, d.sin), (icos, d.icos), (isin, d.isin)):
                act.dma_start(t[:], s).then_inc(consts, 16)
            act.dma_start(m.subln[:], bc(d.a_subln_gain)).then_inc(consts, 16)
            for g, s in enumerate((d.a_q_norm_gain, d.a_k_norm_gain, d.b_q_norm_gain, d.b_k_norm_gain)):
                act.dma_start(gains[:, g], bc(s)).then_inc(consts, 16)
            for g, s in enumerate((d.a_lambda_q1, d.a_lambda_q2, d.a_lambda_k1, d.a_lambda_k2)):
                act.dma_start(lams[:, g], bc(s)).then_inc(consts, 16)
            act.wait_ge(dve_order, 1)
            for i in range(NT + 1):
                r = rows_of(i)
                act.wait_ge(x_loaded[i], 16)
                src = m.stream[:, i, :] if i < NT else meta[:]
                nc.scalar.activation(raw[0:r].rearrange("p a b -> p (a b)"), src, ACT.Square,
                                     accum_out=sums[0:r, i:i + 1]).then_inc(squared, 1)
                act.wait_ge(squared, i + 1)
            act.wait_ge(lam_dots, 1)
            nc.scalar.activation(lam2[:], lam2[:], ACT.Exp).then_inc(lam_exps, 1)
            act.wait_ge(ms_ready, 1)
            nc.scalar.activation(root[:, 0:NT + 1], ms[:, 0:NT + 1], ACT.Sqrt).then_inc(root_ready, 1)

            dests = {"ak": m.akT, "aq": m.aqT, "iq": m.iqT, "bq": m.bqT}

            def turn_out(q):
                _, kind, i = STEPS[ROT_STEPS[q]]
                r = rows_of(i)
                act.wait_ge(turned, q + 1)
                ps = bank(m, 2 + q % 2).rearrange("p (c t) -> p c t", c=4)[:, :, 0:r]
                key_lo = META + i * P if i < NT else 0
                if kind == "small":
                    nc.scalar.copy(m.bkT[:, key_lo:key_lo + r], ps[:, 0])
                    nc.scalar.copy(m.ikT[:, key_lo:key_lo + r], ps[:, 1]).then_inc(turned_out, 1)
                else:
                    lo = key_lo if kind == "ak" else i * P
                    nc.scalar.copy(dests[kind][:, :, lo:lo + r], ps).then_inc(turned_out, 1)

            gate = 0
            for n, (c, kind, i) in enumerate(STEPS):
                r = rows_of(i)
                act.wait_ge(projected, n + 1)
                ps = bank(m, n % 2)[0:r]
                if kind in ROTATED:
                    q = ROT_STEPS.index(n)
                    if q >= 2:
                        act.wait_ge(rotated, q - 1)
                    w = SMALL if kind == "small" else WIDE
                    nc.scalar.copy(raw[0:r, q % 2, 0:w], ps[:, 0:w]).then_inc(evacuated, 1)
                    if kind != "iq":
                        heads = 1 if kind == "small" else GROUPS
                        k = sum(STEPS[s][1] != "iq" for s in ROT_STEPS[:q + 1])
                        act.wait_ge(head_ms, k)
                        nc.scalar.activation(root[0:r, 0:heads], ms[0:r, 0:heads], ACT.Sqrt).then_inc(head_root, 1)
                elif kind == "av":
                    nc.scalar.copy(m.av[0:r, i], ps).then_inc(evacuated, 1)
                else:
                    g = c - CHUNKS.index("gate")
                    nc.scalar.activation(m.gates[:, i, g * WIDE:(g + 1) * WIDE], ps, ACT.Sigmoid).then_inc(evacuated, 1)
                if n - 1 in ROT_STEPS:
                    turn_out(ROT_STEPS.index(n - 1))

        @block.tensor
        def _(pe):
            for i in range(NT + 1):
                r = rows_of(i)
                pe.wait_ge(xn_ready, i + 1)
                if i >= 1:
                    pe.wait_ge(xT_ready, i)
                for c in range(DC):
                    last = nc.tensor.transpose(bank(m, 6, 2)[:, c * P:c * P + r], xn[0:r, c * P:(c + 1) * P],
                                               m.ident[0:r, 0:r])
                last.then_inc(xn_turned, 1)
            pe.wait_ge(xT_ready, NT + 1)

            def turn(q):
                _, kind, i = STEPS[ROT_STEPS[q]]
                r = rows_of(i)
                pe.wait_ge(rotated, q + 1)
                if q >= 2:
                    pe.wait_ge(turned_out, q - 1)
                blocks = 2 if kind == "small" else 4
                for b in range(blocks):
                    last = nc.tensor.transpose(bank(m, 2 + q % 2)[:, b * P:b * P + r],
                                               rot[0:r, q % 2, b * P:(b + 1) * P], m.ident[0:r, 0:r])
                last.then_inc(turned, 1)

            for n, (c, kind, i) in enumerate(STEPS):
                r = rows_of(i)
                if i == 0:
                    pe.wait_ge(w_loaded[c % 2], 16 * (c // 2 + 1))
                if n >= 2:
                    pe.wait_ge(evacuated, n - 1)
                w = SMALL if kind == "small" else WIDE
                lo = META + i * P if i < NT else 0
                for k in range(DC):
                    last = nc.tensor.matmul(bank(m, n % 2)[0:r, 0:w], xT[:, k, lo:lo + r], wch[:, c % 2, k, 0:w],
                                            start=(k == 0), stop=(k == DC - 1))
                last.then_inc(projected, 1)
                if n - 1 in ROT_STEPS:
                    turn(ROT_STEPS.index(n - 1))


UNITS = A_HEADS + B_HEADS
ROUNDS = TOPK // 8


def keys_of(i):
    return META + (i + 1) * P


def blocks_of(i):
    return [(META + b * P, P, b, b * P) for b in range(i + 1)] + [(0, META, NT, NT * P)]


def score_plan():
    plan = []
    for i in range(NT):
        plan += [(i, "idx", h, 0) for h in range(IDX_HEADS)]
        plan += [(i, "a", h, s) for h in range(A_HEADS) for s in range(2)]
        plan += [(i, "b", h, 0) for h in range(B_HEADS)]
    return plan


PLAN = score_plan()
SCORE = {key: n for n, key in enumerate(PLAN)}


def softmaxes_before(i, kind, h, s=0):
    return i * (2 * A_HEADS + B_HEADS) + (2 * h + s if kind == "a" else 2 * A_HEADS + h)


def attend(nc, m, d):
    w_out = placer(nc, m.free0)("w_out", [P, DC, D])
    sb = placer(nc, m.free2)
    w_a = sb("w_a", [P, 4, D])
    w_b = sb("w_b", [P, 4, D])
    probs = sb("probs", [P, 4, KEYS])
    pT = sb("pT", [P, 2, (NT + 1) * P])
    score = sb("score", [P, KEYS])
    bias = sb("bias", [P, KEYS], BF16)
    maxima = sb("maxima", [P, ROUNDS, 8])
    nmax = sb("nmax", [P, 16])
    total = sb("total", [P, 16])
    ratio = sb("ratio", [P, A_HEADS])
    recip = sb("recip", [P, 12])
    ms = sb("ms_s", [P, A_HEADS])
    root = sb("root_s", [P, A_HEADS])
    inv = sb("inv_s", [P, A_HEADS])
    out_a = sb("out_a", [P, WIDE])
    out_b = sb("out_b", [P, WIDE])
    sq = sb("sq_s", [P, WIDE])
    outT = sb("outT", [P, 8, P])
    mixed = sb("mixed", [P, D])
    relu_ring = [sb("relu0", [P, KEYS]), sb("relu1", [P, KEYS])]

    weights = nc.alloc_semaphore("weights_b")
    scored = nc.alloc_semaphore("scored")
    scores_used = nc.alloc_semaphore("scores_used")
    max_ready = nc.alloc_semaphore("max_ready")
    idx_added = nc.alloc_semaphore("idx_added")
    bias_ready = nc.alloc_semaphore("bias_ready")
    combined = nc.alloc_semaphore("combined")
    p_turned = nc.alloc_semaphore("p_turned")
    pT_ready = nc.alloc_semaphore("pT_ready")
    valued = nc.alloc_semaphore("valued")
    outs_read = nc.alloc_semaphore("outs_read")
    sub_ms = nc.alloc_semaphore("sub_ms")
    sub_root = nc.alloc_semaphore("sub_root")
    outs_ready = nc.alloc_semaphore("outs_ready")
    outs_turned = nc.alloc_semaphore("outs_turned")
    outT_ready = nc.alloc_semaphore("outT_ready")
    branched = nc.alloc_semaphore("branched")
    mixed_ready = nc.alloc_semaphore("mixed_ready")
    mixed_turned = nc.alloc_semaphore("mixed_turned")
    mixedT_ready = nc.alloc_semaphore("mixedT_ready")
    outed = nc.alloc_semaphore("outed")
    streamed = nc.alloc_semaphore("streamed")
    dve_order = nc.alloc_semaphore("dve_order_b")

    def unit(i, kind, h):
        return i * UNITS + (h if kind == "a" else A_HEADS + h)

    with nc.Block() as block:
        @block.sync
        def _(sp):
            sp.dma_start(w_a[:], d.w_branch_a).then_inc(weights, 16)
            sp.dma_start(w_b[:], d.w_branch_b).then_inc(weights, 16)
            sp.dma_start(w_out[:], d.w_out).then_inc(weights, 16)

        @block.tensor
        def _(pe):
            def score_of(i, kind, h, s):
                n = SCORE[(i, kind, h, s)]
                w = keys_of(i)
                if n >= 2:
                    pe.wait_ge(scores_used, n - 1)
                if kind == "idx":
                    lo, block_, q, k = HEAD * (h % 2), h // 2, m.iqT, m.ikT[:]
                elif kind == "a":
                    lo, block_, q, k = HEAD * s, h, m.aqT, m.akT[:, h]
                else:
                    lo, block_, q, k = HEAD * (h % 2), h // 2, m.bqT, m.bkT[:]
                    pe.wait_ge(bias_ready, i + 1)
                ps = bank(m, 2 * (n % 2), 2)
                hi = lo + HEAD
                for c in range(0, w, 512):
                    e = min(w, c + 512)
                    plain = kind == "idx"
                    last = nc.tensor.matmul(ps[:, c:e], q[lo:hi, block_, i * P:(i + 1) * P], k[lo:hi, c:e],
                                            start=True, stop=plain, skip_group_check=True)
                    if kind == "b":
                        last = nc.tensor.matmul(ps[:, c:e], m.ident_b[:], bias[:, c:e], start=False, stop=True,
                                                skip_group_check=True)
                if kind == "a":
                    for c in range(0, w, 512):
                        f, e = max(c, w - P), min(w, c + 512)
                        if f < e:
                            last = nc.tensor.matmul(ps[:, f:e], m.ident_b[:], m.tri_b[:, f - (w - P):e - (w - P)],
                                                    start=False, stop=True, skip_group_check=True)
                last.then_inc(scored, 1)

            def turn(i, kind, h):
                u = unit(i, kind, h)
                if kind == "a":
                    pe.wait_ge(combined, i * A_HEADS + h + 1)
                    p = probs[:, 2 * (h % 2)]
                else:
                    pe.wait_ge(scores_used, SCORE[(i, "b", h, 0)] + 1)
                    p = probs[:, h % 4]
                if u >= 1:
                    pe.wait_ge(pT_ready, u)
                for key, n, _, col in blocks_of(i):
                    last = nc.tensor.transpose(bank(m, 4, 2)[0:n, col:col + P], p[:, key:key + n], m.ident[:])
                last.then_inc(p_turned, 1)

            def value(i, kind, h):
                u = unit(i, kind, h)
                pe.wait_ge(pT_ready, u + 1)
                if h == 0 and i >= 1:
                    pe.wait_ge(outs_read, i)
                blocks = blocks_of(i)
                for k, (_, n, t, col) in enumerate(blocks):
                    if kind == "a":
                        dst, v = bank(m, 6)[:, h * P:(h + 1) * P], m.av[0:n, t, h * P:(h + 1) * P]
                    else:
                        dst, v = bank(m, 7)[:, h * HEAD:(h + 1) * HEAD], m.bv[0:n, t]
                    last = nc.tensor.matmul(dst, pT[0:n, u % 2, col:col + P], v,
                                            start=(k == 0), stop=(k == len(blocks) - 1), skip_group_check=True)
                last.then_inc(valued, 1)

            def output(i):
                if i == 0:
                    pe.wait_ge(weights, 48)
                done = SCORE[(i + 1, "idx", IDX_HEADS - 1, 0)] + 1 if i + 1 < NT else len(PLAN)
                pe.wait_ge(scores_used, done)
                pe.wait_ge(pT_ready, (i + 1) * UNITS)
                pe.wait_ge(outs_read, i + 1)
                for br, src in ((1, out_b), (0, out_a)):
                    if br == 0:
                        pe.wait_ge(outs_ready, i + 1)
                    for c in range(4):
                        last = nc.tensor.transpose(bank(m, 4 + br)[:, c * P:(c + 1) * P],
                                                   src[:, c * P:(c + 1) * P], m.ident[:])
                    last.then_inc(outs_turned, 1)
                for k, (br, w) in enumerate(((1, w_b), (0, w_a))):
                    pe.wait_ge(outT_ready, 2 * i + k + 1)
                    for half in range(2):
                        for c in range(4):
                            last = nc.tensor.matmul(bank(m, 2 * br + half), outT[:, 4 * br + c, :],
                                                    w[:, c, half * 512:(half + 1) * 512],
                                                    start=(c == 0), stop=(c == 3))
                    last.then_inc(branched, 1)
                pe.wait_ge(mixed_ready, i + 1)
                for c in range(DC):
                    last = nc.tensor.transpose(bank(m, 4, 2)[:, c * P:(c + 1) * P], mixed[:, c * P:(c + 1) * P],
                                               m.ident[:])
                last.then_inc(mixed_turned, 1)
                pe.wait_ge(mixedT_ready, i + 1)
                for half in range(2):
                    for c in range(DC):
                        last = nc.tensor.matmul(bank(m, half), outT[:, c, :], w_out[:, c, half * 512:(half + 1) * 512],
                                                start=(c == 0), stop=(c == DC - 1))
                last.then_inc(outed, 1)

            for i in range(NT):
                for h in range(IDX_HEADS):
                    score_of(i, "idx", h, 0)
                if i >= 1:
                    output(i - 1)
                    pe.wait_ge(streamed, i)
                units = [("a", h) for h in range(A_HEADS)] + [("b", h) for h in range(B_HEADS)]
                for k in range(UNITS + 2):
                    if k < UNITS:
                        kind, h = units[k]
                        for s in range(2 if kind == "a" else 1):
                            score_of(i, kind, h, s)
                    if 1 <= k <= UNITS:
                        turn(i, *units[k - 1])
                    if k >= 2:
                        value(i, *units[k - 2])
            output(NT - 1)

        @block.scalar
        def _(act):
            def turn_out(u, i):
                act.wait_ge(p_turned, u + 1)
                if u >= 2:
                    act.wait_ge(valued, u - 1)
                nc.scalar.copy(pT[:, u % 2, 0:(i + 1) * P], bank(m, 4)[:, 0:(i + 1) * P])
                nc.scalar.copy(pT[0:META, u % 2, NT * P:], bank(m, 5)[0:META, 0:P]).then_inc(pT_ready, 1)

            def exp_of(i, kind, h, s):
                n = SCORE[(i, kind, h, s)]
                w = keys_of(i)
                j = softmaxes_before(i, kind, h, s)
                act.wait_ge(max_ready, j + 1)
                u = unit(i, kind, h)
                if u >= 2:
                    act.wait_ge(p_turned, u - 1)
                slot = 2 * (h % 2) + s if kind == "a" else h % 4
                jj = j % 16
                nc.scalar.activation(probs[:, slot, 0:w], bank(m, 2 * (n % 2), 2)[:, 0:w], ACT.Exp,
                                     bias=nmax[:, jj:jj + 1], accum_out=total[:, jj:jj + 1]).then_inc(scores_used, 1)

            def output(i):
                act.wait_ge(sub_ms, i + 1)
                nc.scalar.activation(root[:], ms[:], ACT.Sqrt).then_inc(sub_root, 1)
                if i >= 1:
                    act.wait_ge(outed, i)
                for k, br in enumerate((1, 0)):
                    act.wait_ge(outs_turned, 2 * i + k + 1)
                    nc.scalar.copy(outT[:, 4 * br:4 * br + 4, :].rearrange("p c t -> p (c t)"),
                                   bank(m, 4 + br)).then_inc(outT_ready, 1)
                act.wait_ge(mixed_turned, i + 1)
                act.wait_ge(branched, 2 * i + 2)
                nc.scalar.copy(outT[:].rearrange("p c t -> p (c t)"), bank(m, 4, 2)).then_inc(mixedT_ready, 1)

            for i in range(NT):
                w = keys_of(i)
                for h in range(IDX_HEADS):
                    n = SCORE[(i, "idx", h, 0)]
                    act.wait_ge(scored, n + 1)
                    if i * IDX_HEADS + h >= 2:
                        act.wait_ge(idx_added, i * IDX_HEADS + h - 1)
                    nc.scalar.activation(relu_ring[h % 2][:, 0:w], bank(m, 2 * (n % 2), 2)[:, 0:w],
                                         ACT.Relu).then_inc(scores_used, 1)
                if i >= 1:
                    output(i - 1)
                units = [("a", h) for h in range(A_HEADS)] + [("b", h) for h in range(B_HEADS)]
                for k in range(UNITS + 1):
                    if k < UNITS:
                        kind, h = units[k]
                        for s in range(2 if kind == "a" else 1):
                            exp_of(i, kind, h, s)
                    if k >= 1:
                        turn_out(unit(i, *units[k - 1]), i)
            output(NT - 1)

        @block.vector
        def _(dve):
            link = chain(dve, dve_order)

            def rounds(i, n):
                w = keys_of(i)
                for _ in range(n):
                    r = round_[0]
                    round_[0] += 1
                    link(nc.vector.max(maxima[:, r], score[:, 0:w]))
                    link(nc.vector.match_replace(score[:, 0:w], maxima[:, r], score[:, 0:w], TAKEN))

            def max_of(i, kind, h, s):
                n = SCORE[(i, kind, h, s)]
                jj = softmaxes_before(i, kind, h, s) % 16
                dve.wait_ge(scored, n + 1)
                nc.vector.tensor_reduce(nmax[:, jj:jj + 1], bank(m, 2 * (n % 2), 2)[:, 0:keys_of(i)], X, ALU.max,
                                        negate=True).then_inc(max_ready, 1)

            def output(i, n_rounds):
                dve.wait_ge(valued, (i + 1) * UNITS)
                for h in range(A_HEADS):
                    nc.vector.tensor_scalar(out_a[:, h * P:(h + 1) * P], bank(m, 6)[:, h * P:(h + 1) * P],
                                            recip[:, h:h + 1], None, ALU.mult)
                nc.vector.tensor_tensor(out_b[:].rearrange("p (h w) -> p h w", h=B_HEADS),
                                        bank(m, 7).rearrange("p (h w) -> p h w", h=B_HEADS),
                                        bcast(recip[:, A_HEADS:], 2, HEAD), ALU.mult).then_inc(outs_read, 1)
                dve.wait_ge(outs_read, i + 1)
                link(nc.vector.tensor_tensor(sq[:], out_a[:], out_a[:], ALU.mult))
                link(nc.vector.tensor_reduce(ms[:], sq[:].rearrange("p (h w) -> p h w", h=A_HEADS), X, ALU.add))
                nc.vector.tensor_scalar(ms[:], ms[:], 1.0 / P, EPS, ALU.mult, ALU.add).then_inc(sub_ms, 1)
                dve.wait_ge(sub_root, i + 1)
                inverse_root(nc, link, inv[:], root[:], ms[:])
                a3 = out_a[:].rearrange("p (h w) -> p h w", h=A_HEADS)
                link(nc.vector.tensor_tensor(a3, a3, bcast(inv[:], 2, P), ALU.mult))
                nc.vector.tensor_tensor(a3, a3, bcast(m.subln[:], 1, A_HEADS), ALU.mult).then_inc(outs_ready, 1)
                rounds(i + 1, n_rounds)
                ga, gb = m.gates[:, i, 0:D], m.gates[:, i, D:]
                dve.wait_ge(branched, 2 * i + 1)
                link(nc.vector.tensor_tensor(gb, gb, bank(m, 2, 2), ALU.mult))
                dve.wait_ge(branched, 2 * i + 2)
                link(nc.vector.tensor_tensor(ga, ga, bank(m, 0, 2), ALU.mult))
                nc.vector.tensor_tensor(mixed[:], ga, gb, ALU.add).then_inc(mixed_ready, 1)
                rounds(i + 1, n_rounds)
                dve.wait_ge(outed, i + 1)
                nc.vector.tensor_tensor(m.stream[:, i, :], m.stream[:, i, :], bank(m, 0, 2),
                                        ALU.add).then_inc(streamed, 1)

            round_ = [0]
            for i in range(NT):
                w = keys_of(i)
                round_[0] = 0
                for h in range(IDX_HEADS):
                    dve.wait_ge(scores_used, SCORE[(i, "idx", h, 0)] + 1)
                    r = relu_ring[h % 2][:, 0:w]
                    if h == 0:
                        ins = nc.vector.tensor_scalar(score[:, 0:w], r, m.iw[:, i, 0:1], None, ALU.mult)
                    else:
                        ins = nc.vector.scalar_tensor_tensor(score[:, 0:w], r, m.iw[:, i, h:h + 1], score[:, 0:w],
                                                             ALU.mult, ALU.add)
                    ins.then_inc(idx_added, 1)
                    dve.wait_ge(idx_added, i * IDX_HEADS + h + 1)
                link(nc.vector.tensor_tensor(score[:, w - P:w], score[:, w - P:w], m.tri[:], ALU.add))
                if i >= 1:
                    output(i - 1, 4)
                left = (ROUNDS - round_[0]) // A_HEADS
                for h in range(A_HEADS):
                    max_of(i, "a", h, 0)
                    max_of(i, "a", h, 1)
                    rounds(i, left)
                    dve.wait_ge(scores_used, SCORE[(i, "a", h, 1)] + 1)
                    link(nc.vector.reciprocal(ratio[:, h:h + 1], total[:, 2 * h + 1:2 * h + 2]))
                    link(nc.vector.tensor_scalar(ratio[:, h:h + 1], ratio[:, h:h + 1], total[:, 2 * h:2 * h + 1],
                                                 m.neg_lam[:, 0:1], ALU.mult, ALU.mult))
                    nc.vector.reciprocal(recip[:, h:h + 1], total[:, 2 * h:2 * h + 1])
                    s0 = 2 * (h % 2)
                    nc.vector.scalar_tensor_tensor(probs[:, s0, 0:w], probs[:, s0 + 1, 0:w], ratio[:, h:h + 1],
                                                   probs[:, s0, 0:w], ALU.mult, ALU.add).then_inc(combined, 1)
                link(nc.vector.tensor_scalar(score[:, 0:w], score[:, 0:w], 2 * UNSEEN, MASKED, ALU.is_gt, ALU.mult))
                link(nc.vector.tensor_tensor(score[:, w - P:w], score[:, w - P:w], m.tri_b[:], ALU.add))
                nc.vector.tensor_copy(bias[:, 0:w], score[:, 0:w]).then_inc(bias_ready, 1)
                for h in range(B_HEADS):
                    max_of(i, "b", h, 0)
                dve.wait_ge(scores_used, SCORE[(i, "b", B_HEADS - 1, 0)] + 1)
                link(nc.vector.reciprocal(recip[:, A_HEADS:], total[:, 2 * A_HEADS:]))
            output(NT - 1, 0)


HOT = 4
HOT_TURNS = P // (2 * HOT)


def route(nc, m, d):
    sb = placer(nc, m.free1)
    wq = sb("wq", [P, DC, D])
    keysT = sb("keysT", [P, PEER_HEADS, N_KEYS])
    stage = sb("stage", [P, N_KEYS, P])
    hn = sb("hn", [P, D])
    hnT = sb("hnT", [P, DC, P])
    q_sb = sb("q_sb", [P, D])
    qT = sb("qT", [P, PEER_HEADS, P])
    s_sb = sb("s_sb", [P, 2 * PEER_HEADS, N_KEYS])
    sums = sb("sums_r", [P, NT])
    root = sb("root_r", [P, 1])
    ms = sb("ms_r", [P, 1])
    val = sb("val", [P, 2 * PEER_HEADS, PEER_TOPK])
    idx = sb("idx", [P, 2 * PEER_HEADS, PEER_TOPK], U32)
    idx_f = sb("idx_f", [P, 2 * PEER_HEADS, PEER_TOPK])
    cand = sb("cand", [P, PEER_HEADS, CANDS])
    code = sb("code", [P, PEER_HEADS, CANDS])
    top = sb("top", [P, PEER_HEADS, PEER_TOPK])
    top_at = sb("top_at", [P, PEER_HEADS, PEER_TOPK], U32)
    top_at_f = sb("top_at_f", [P, PEER_HEADS, PEER_TOPK])
    hits = sb("hits", [P, 2, PEER_TOPK, CANDS])
    pick = sb("pick", [P, PEER_HEADS, PEER_TOPK])
    pick_i = sb("pick_i", [P, 3, PICKS], I32)
    picks = sb("picks", [P, 3, PICKS])
    norm = sb("norm", [P, PEER_HEADS])
    picksT = sb("picksT", [P, 2, 3, P])
    hot_i = sb("hot_i", [P, 2, HOT, N_KEYS])
    hot_j = sb("hot_j", [P, 2, HOT, N_KEYS])

    names = ("weights_c squared_c ms_ready_c root_ready_c hn_ready hn_turned hnT_ready queried q_out q_turned "
             "qT_ready routed s_out s_read shifted exped hit_ready hit_coded picks_ready picks_turned picksT_ready "
             "hot_ready hot_used gate_out stage_stored dve_order_c").split()
    s = {n: nc.alloc_semaphore(n) for n in names}

    with nc.Block() as block:
        @block.sync
        def _(sp):
            sp.dma_start(wq[:], d.w_query).then_inc(s["weights_c"], 16)
            sp.dma_start(keysT[:], d.sub_keys).then_inc(s["weights_c"], 16)
            for i in range(NT):
                sp.wait_ge(s["gate_out"], 2 + (i + 1) * P // HOT)
                sp.dma_start(d.gate_mat[:, :, i * P:(i + 1) * P].rearrange("j i t -> i j t"),
                             stage[:]).then_inc(s["stage_stored"], 16)
            sp.wait_ge(s["stage_stored"], 16 * NT)

        @block.tensor
        def _(pe):
            pe.sem_inc(s["hot_used"], 2)

            def score(i):
                pe.wait_ge(s["hn_ready"], i + 1)
                if i >= 1:
                    pe.wait_ge(s["s_out"], i)
                for c in range(DC):
                    last = nc.tensor.transpose(bank(m, 0, 2)[:, c * P:(c + 1) * P], hn[:, c * P:(c + 1) * P], m.ident[:])
                last.then_inc(s["hn_turned"], 1)
                if i == 0:
                    pe.wait_ge(s["weights_c"], 32)
                pe.wait_ge(s["hnT_ready"], i + 1)
                for half in range(2):
                    for c in range(DC):
                        last = nc.tensor.matmul(bank(m, 2 + half), hnT[:, c, :], wq[:, c, half * 512:(half + 1) * 512],
                                                start=(c == 0), stop=(c == DC - 1))
                last.then_inc(s["queried"], 1)
                pe.wait_ge(s["q_out"], i + 1)
                for h in range(PEER_HEADS):
                    last = nc.tensor.transpose(bank(m, 4, 2)[:, h * P:(h + 1) * P], q_sb[:, h * P:(h + 1) * P], m.ident[:])
                last.then_inc(s["q_turned"], 1)
                pe.wait_ge(s["qT_ready"], i + 1)
                for h in range(PEER_HEADS):
                    for c in range(2):
                        lo = c * HEAD
                        last = nc.tensor.matmul(bank(m, 2 * c, 2)[:, h * P:(h + 1) * P],
                                                qT[lo:lo + HEAD, h, :], keysT[lo:lo + HEAD, h, :],
                                                start=True, stop=True, skip_group_check=True)
                last.then_inc(s["routed"], 1)

            def gates(i):
                pe.wait_ge(s["picks_ready"], i + 1)
                for k in range(3):
                    last = nc.tensor.transpose(bank(m, 4)[:, k * P:(k + 1) * P], picks[:, k], m.ident[:])
                last.then_inc(s["picks_turned"], 1)
                with pe.Fori(0, HOT_TURNS) as turn:
                    for b in range(2):
                        n = turn * 2 + (i * 2 * HOT_TURNS + b + 1)
                        pe.wait_ge(s["hot_ready"], n)
                        pe.wait_ge(s["gate_out"], n)
                        for t in range(HOT):
                            last = nc.tensor.matmul(bank(m, 6 + b)[:, t * P:(t + 1) * P], hot_i[:, b, t], hot_j[:, b, t],
                                                    start=True, stop=True, skip_group_check=True)
                        last.then_inc(s["hot_used"], 1)

            score(0)
            for i in range(NT):
                if i + 1 < NT:
                    score(i + 1)
                gates(i)

        @block.scalar
        def _(act):
            act.sem_inc(s["gate_out"], 2)

            def score(i):
                if i >= 1:
                    act.wait_ge(s["hn_turned"], i)
                    act.wait_ge(s["q_turned"], i)
                nc.scalar.activation(q_sb[:], m.stream[:, i, :], ACT.Square,
                                     accum_out=sums[:, i:i + 1]).then_inc(s["squared_c"], 1)
                act.wait_ge(s["ms_ready_c"], i + 1)
                nc.scalar.activation(root[:], ms[:], ACT.Sqrt).then_inc(s["root_ready_c"], 1)
                act.wait_ge(s["queried"], i + 1)
                nc.scalar.copy(q_sb[:], bank(m, 2, 2)).then_inc(s["q_out"], 1)
                act.wait_ge(s["q_turned"], i + 1)
                nc.scalar.copy(qT[:].rearrange("p h t -> p (h t)"), bank(m, 4, 2)).then_inc(s["qT_ready"], 1)
                act.wait_ge(s["routed"], i + 1)
                if i >= 1:
                    act.wait_ge(s["s_read"], i)
                nc.scalar.copy(s_sb[:].rearrange("p h k -> p (h k)"), bank(m, 0, 4)).then_inc(s["s_out"], 1)

            def gates(i):
                act.wait_ge(s["shifted"], i + 1)
                nc.scalar.activation(top[:], top[:], ACT.Exp).then_inc(s["exped"], 1)
                act.wait_ge(s["picks_turned"], i + 1)
                nc.scalar.copy(picksT[:, i % 2].rearrange("p a t -> p (a t)"),
                               bank(m, 4)[:, 0:3 * P]).then_inc(s["picksT_ready"], 1)
                if i >= 1:
                    act.wait_ge(s["stage_stored"], 16 * i)
                with act.Fori(0, HOT_TURNS) as turn:
                    for b in range(2):
                        act.wait_ge(s["hot_used"], turn * 2 + (i * 2 * HOT_TURNS + b + 3))
                        nc.scalar.copy(stage[:, :, bass.ds(turn * (2 * HOT) + b * HOT, HOT)].rearrange("p j t -> p t j"),
                                       bank(m, 6 + b).rearrange("p (t j) -> p t j", t=HOT)).then_inc(s["gate_out"], 1)

            score(0)
            for i in range(NT):
                if i + 1 < NT:
                    score(i + 1)
                gates(i)

        @block.gpsimd
        def _(pool):
            for i in range(NT):
                for h in range(PEER_HEADS):
                    pool.wait_ge(s["hit_ready"], i * PEER_HEADS + h + 1)
                    nc.gpsimd.tensor_tensor(hits[:, h % 2], hits[:, h % 2], bcast(code[:, h], 1, PEER_TOPK),
                                            ALU.mult).then_inc(s["hit_coded"], 1)

        @block.vector
        def _(dve):
            link = chain(dve, s["dve_order_c"])

            def normed(i):
                dve.wait_ge(s["squared_c"], i + 1)
                nc.vector.tensor_scalar(ms[:], sums[:, i:i + 1], 1.0 / D, EPS, ALU.mult, ALU.add).then_inc(s["ms_ready_c"], 1)
                dve.wait_ge(s["root_ready_c"], i + 1)
                inverse_root(nc, link, sums[:, i:i + 1], root[:], ms[:])
                if i >= 1:
                    dve.wait_ge(s["hn_turned"], i)
                nc.vector.tensor_scalar(hn[:], m.stream[:, i, :], sums[:, i:i + 1], None, ALU.mult).then_inc(s["hn_ready"], 1)
                dve.wait_ge(s["hn_turned"], i + 1)
                if i >= 1:
                    dve.wait_ge(s["queried"], i)
                nc.vector.tensor_tensor(hnT[:], bank(m, 0, 2).rearrange("p (c t) -> p c t", c=DC),
                                        bcast(m.ffn_gain[:], 2, P), ALU.mult).then_inc(s["hnT_ready"], 1)
                dve.wait_ge(s["hnT_ready"], i + 1)
                part = slice(i * P, (i + 1) * P)
                link(nc.vector.tensor_copy(m.xh[:, :, part], hnT[:]))
                link(nc.vector.tensor_tensor(m.xl[:, :, part], hnT[:], m.xh[:, :, part].bitcast(F32), ALU.subtract))

            def search(values, where, src):
                link(nc.vector.max(values[:, 0:8], src))
                link(nc.vector.max_index(where[:, 0:8], values[:, 0:8], src))
                link(nc.vector.match_replace(src, values[:, 0:8], src, TAKEN))
                link(nc.vector.max(values[:, 8:16], src))
                return nc.vector.max_index(where[:, 8:16], values[:, 8:16], src)

            def pairs(out, part):
                first, second = part[:, 0:PEER_HEADS], part[:, PEER_HEADS:]
                at, a = 0, 0
                while a < PEER_TOPK:
                    n = ROWS[a][1]
                    k = sum(r[1] == n for r in ROWS)
                    dst = out[:, :, at:at + k * n].rearrange("p h (a b) -> p h a b", b=n)
                    last = nc.vector.tensor_tensor(dst, bcast(second[:, :, 0:n], 2, k), bcast(first[:, :, a:a + k], 3, n),
                                                   ALU.add)
                    at, a = at + k * n, a + k
                return last

            def chosen(i):
                dve.wait_ge(s["s_out"], i + 1)
                for ch in range(2 * PEER_HEADS):
                    last = search(val[:, ch], idx[:, ch], s_sb[:, ch])
                    if ch < 2 * PEER_HEADS - 1:
                        link(last)
                last.then_inc(s["s_read"], 1)
                dve.wait_ge(s["s_read"], i + 1)
                link(nc.vector.tensor_copy(idx_f[:], idx[:]))
                rows = idx_f[:, 0:PEER_HEADS]
                link(nc.vector.tensor_scalar(rows, rows, float(N_KEYS), None, ALU.mult))
                link(pairs(cand, val[:]))
                link(pairs(code, idx_f[:]))
                for h in range(PEER_HEADS):
                    link(search(top[:, h], top_at[:, h], cand[:, h]))
                link(nc.vector.tensor_copy(top_at_f[:], top_at[:]))
                link(nc.vector.tensor_copy(norm[:], top[:, :, 0]))
                nc.vector.tensor_tensor(top[:], top[:], bcast(norm[:], 2, PEER_TOPK), ALU.subtract).then_inc(s["shifted"], 1)
                for h in range(PEER_HEADS):
                    n = i * PEER_HEADS + h
                    nc.vector.tensor_tensor(hits[:, h % 2], bcast(top_at_f[:, h], 2, CANDS),
                                            bcast(m.iota[:, 0:CANDS], 1, PEER_TOPK), ALU.is_equal).then_inc(s["hit_ready"], 1)
                    if h >= 1:
                        dve.wait_ge(s["hit_coded"], n)
                        link(nc.vector.tensor_reduce(pick[:, h - 1], hits[:, (h - 1) % 2], X, ALU.add))
                dve.wait_ge(s["hit_coded"], (i + 1) * PEER_HEADS)
                link(nc.vector.tensor_reduce(pick[:, PEER_HEADS - 1], hits[:, (PEER_HEADS - 1) % 2], X, ALU.add))
                link(nc.vector.tensor_copy(pick_i[:, 2], pick[:].rearrange("p h k -> p (h k)")))
                nc.vector.tensor_scalar(pick_i[:, 0], pick_i[:, 2], 7, None, ALU.logical_shift_right)
                link(nc.vector.tensor_scalar(pick_i[:, 1], pick_i[:, 2], N_KEYS - 1, None, ALU.bitwise_and))
                if i >= 1:
                    dve.wait_ge(s["picks_turned"], i)
                nc.vector.tensor_copy(picks[:, 0:2], pick_i[:, 0:2])
                dve.wait_ge(s["exped"], i + 1)
                link(nc.vector.tensor_reduce(norm[:], top[:], X, ALU.add))
                link(nc.vector.reciprocal(norm[:], norm[:]))
                nc.vector.tensor_tensor(picks[:, 2].rearrange("p (h k) -> p h k", h=PEER_HEADS), top[:],
                                        bcast(norm[:], 2, PEER_TOPK), ALU.mult).then_inc(s["picks_ready"], 1)

            def one_hot(i):
                dve.wait_ge(s["picksT_ready"], i + 1)
                with dve.Fori(0, HOT_TURNS) as turn:
                    for b in range(2):
                        dve.wait_ge(s["hot_used"], turn * 2 + (i * 2 * HOT_TURNS + b + 1))
                        for t in range(HOT):
                            tok = turn * (2 * HOT) + (b * HOT + t)
                            nc.vector.tensor_scalar(hot_i[:, b, t], m.iota[:], picksT[:, i % 2, 0, bass.ds(tok, 1)],
                                                    picksT[:, i % 2, 2, bass.ds(tok, 1)], ALU.is_equal, ALU.mult)
                            last = nc.vector.tensor_scalar(hot_j[:, b, t], m.iota[:], picksT[:, i % 2, 1, bass.ds(tok, 1)],
                                                           None, ALU.is_equal)
                        last.then_inc(s["hot_ready"], 1)

            normed(0)
            for i in range(NT):
                if i + 1 < NT:
                    normed(i + 1)
                chosen(i)
                one_hot(i)


GROUP = 4
N_GROUPS = N_KEYS // GROUP


def experts(nc, m, d):
    sb = placer(nc, m.free1)
    u = sb("u", [P, 2, DC, P])
    uh = sb("uh", [P, 2, DC, P], F32R)
    ul = sb("ul", [P, 2, DC, P], F32R)
    v = sb("v", [P, GROUP, D])
    vh = sb("vh", [P, GROUP, D], F32R)
    vl = sb("vl", [P, GROUP, D], F32R)
    gate = sb("gate", [P, GROUP, SEQ])
    act_w = sb("act_w", [P, 2, SEQ])
    wh = sb("wh", [P, GROUP, SEQ], F32R)
    wl = sb("wl", [P, GROUP, SEQ], F32R)

    u_loaded = [nc.alloc_semaphore(f"u_loaded{k}") for k in range(2)]
    names = ("v_loaded g_loaded u_high u_low v_high v_low activated gated hidden summed added w_high stored").split()
    s = {n: nc.alloc_semaphore(n) for n in names}

    def peeled(engine, body):
        body(0, True)
        with engine.Fori(1, N_GROUPS) as g:
            body(g, False)

    with nc.Block() as block:
        @block.sync
        def _(sp):
            def body(g, first):
                for jj in range(GROUP):
                    n = g * GROUP + jj
                    if not first or jj >= 2:
                        sp.wait_ge(s["u_low"], n - 1)
                    sp.dma_start(u[:, jj % 2], d.u[bass.ds(n, 1)].rearrange("o p c i -> (o p) c i")
                                 ).then_inc(u_loaded[jj % 2], 16)
                    if jj == 1:
                        if not first:
                            sp.wait_ge(s["v_low"], g * GROUP)
                            sp.wait_ge(s["gated"], g * GROUP)
                        sp.dma_start(v[:], d.v[bass.ds(g * GROUP, GROUP)].rearrange("j i n -> i j n")
                                     ).then_inc(s["v_loaded"], 16)
                        sp.dma_start(gate[:], d.gate_mat[bass.ds(g * GROUP, GROUP)].rearrange("j i t -> i j t")
                                     ).then_inc(s["g_loaded"], 16)
            peeled(sp, body)
            for i in range(NT):
                sp.wait_ge(s["added"], (N_GROUPS - 1) * NT + i + 1)
                sp.dma_start(d.out[i * P:(i + 1) * P, :], m.stream[:, i, :]).then_inc(s["stored"], 16)
            sp.wait_ge(s["stored"], 16 * NT)

        @block.tensor
        def _(pe):
            def body(g, first):
                for jj in range(GROUP):
                    n = g * GROUP + jj
                    pe.wait_ge(s["u_low"], n + 1)
                    if not first or jj >= 2:
                        pe.wait_ge(s["activated"], n - 1)
                    for c in range(DC):
                        nc.tensor.matmul(bank(m, jj % 2), uh[:, jj % 2, c], m.xh[:, c], start=(c == 0), stop=False)
                        nc.tensor.matmul(bank(m, jj % 2), uh[:, jj % 2, c], m.xl[:, c], start=False, stop=False)
                        last = nc.tensor.matmul(bank(m, jj % 2), ul[:, jj % 2, c], m.xh[:, c], start=False,
                                                stop=(c == DC - 1))
                    last.then_inc(s["hidden"], 1)
                for i in range(NT):
                    if not first or i >= 2:
                        pe.wait_ge(s["added"], g * NT + i - 1)
                    tok = slice(i * P, (i + 1) * P)
                    for jj in range(GROUP):
                        if i == 0:
                            pe.wait_ge(s["gated"], g * GROUP + jj + 1)
                            pe.wait_ge(s["v_low"], g * GROUP + jj + 1)
                        for lhs, rhss in ((wh, (vh, vl)), (wl, (vh,))):
                            for r, rhs in enumerate(rhss):
                                for half in range(2):
                                    first_mm = jj == 0 and lhs is wh and r == 0
                                    last_mm = jj == GROUP - 1 and lhs is wl
                                    last = nc.tensor.matmul(bank(m, 4 + 2 * (i % 2) + half), lhs[:, jj, tok],
                                                            rhs[:, jj, half * 512:(half + 1) * 512],
                                                            start=first_mm, stop=last_mm)
                    last.then_inc(s["summed"], 1)
            peeled(pe, body)

        @block.scalar
        def _(act):
            def body(g, first):
                def u_high(jj):
                    act.wait_ge(u_loaded[jj % 2], g * (16 * GROUP // 2) + 16 * (jj // 2 + 1))
                    if not first or jj >= 2:
                        act.wait_ge(s["hidden"], g * GROUP + jj - 1)
                    nc.scalar.copy(uh[:, jj % 2], u[:, jj % 2]).then_inc(s["u_high"], 1)

                def v_high(jj):
                    if jj == 0:
                        act.wait_ge(s["v_loaded"], g * 16 + 16)
                        if not first:
                            act.wait_ge(s["summed"], g * NT)
                    nc.scalar.copy(vh[:, jj], v[:, jj]).then_inc(s["v_high"], 1)

                def gelu(jj):
                    n = g * GROUP + jj
                    act.wait_ge(s["hidden"], n + 1)
                    if not first or jj >= 2:
                        act.wait_ge(s["gated"], n - 1)
                    nc.scalar.activation(act_w[:, jj % 2], bank(m, jj % 2), ACT.Gelu).then_inc(s["activated"], 1)

                u_high(0)
                u_high(1)
                v_high(0)
                v_high(1)
                gelu(0)
                u_high(2)
                v_high(2)
                gelu(1)
                u_high(3)
                v_high(3)
                gelu(2)
                gelu(3)
            peeled(act, body)

        @block.vector
        def _(dve):
            def add(g, i):
                dve.wait_ge(s["summed"], g * NT + i + 1)
                nc.vector.tensor_tensor(m.stream[:, i, :], m.stream[:, i, :], bank(m, 4 + 2 * (i % 2), 2),
                                        ALU.add).then_inc(s["added"], 1)

            def body(g, first):
                def u_low(jj):
                    n = g * GROUP + jj
                    dve.wait_ge(s["u_high"], n + 1)
                    nc.vector.tensor_tensor(ul[:, jj % 2], u[:, jj % 2], uh[:, jj % 2].bitcast(F32),
                                            ALU.subtract).then_inc(s["u_low"], 1)

                def v_low(jj):
                    dve.wait_ge(s["v_high"], g * GROUP + jj + 1)
                    nc.vector.tensor_tensor(vl[:, jj], v[:, jj], vh[:, jj].bitcast(F32),
                                            ALU.subtract).then_inc(s["v_low"], 1)

                def gated(jj):
                    n = g * GROUP + jj
                    if jj == 0:
                        dve.wait_ge(s["g_loaded"], g * 16 + 16)
                    dve.wait_ge(s["activated"], n + 1)
                    w = gate[:, jj]
                    nc.vector.tensor_tensor(w, w, act_w[:, jj % 2], ALU.mult).then_inc(s["w_high"], 1)
                    dve.wait_ge(s["w_high"], 2 * n + 1)
                    nc.vector.tensor_copy(wh[:, jj], w).then_inc(s["w_high"], 1)
                    dve.wait_ge(s["w_high"], 2 * n + 2)
                    nc.vector.tensor_tensor(wl[:, jj], w, wh[:, jj].bitcast(F32), ALU.subtract).then_inc(s["gated"], 1)

                if not first:
                    add(g - 1, 0)
                    add(g - 1, 1)
                    add(g - 1, 2)
                u_low(0)
                u_low(1)
                if not first:
                    add(g - 1, 3)
                v_low(0)
                v_low(1)
                gated(0)
                u_low(2)
                v_low(2)
                gated(1)
                u_low(3)
                v_low(3)
                gated(2)
                gated(3)
            peeled(dve, body)
            for i in range(NT):
                add(N_GROUPS - 1, i)


class Dram:

    def __init__(self, t):
        self.x, self.meta_tokens = t["x"], t["meta_tokens"]
        self.w_wide, self.w_small = t["w_wide"], t["w_small"]
        self.mix_gain, self.ffn_gain = t["mix_gain"], t["ffn_gain"]
        self.cos, self.sin, self.icos, self.isin = t["cos"], t["sin"], t["icos"], t["isin"]
        self.a_q_norm_gain, self.a_k_norm_gain = t["a_q_norm_gain"], t["a_k_norm_gain"]
        self.b_q_norm_gain, self.b_k_norm_gain = t["b_q_norm_gain"], t["b_k_norm_gain"]
        self.a_subln_gain = t["a_subln_gain"]
        self.a_lambda_q1, self.a_lambda_k1 = t["a_lambda_q1"], t["a_lambda_k1"]
        self.a_lambda_q2, self.a_lambda_k2 = t["a_lambda_q2"], t["a_lambda_k2"]
        self.w_branch_a, self.w_branch_b, self.w_out = t["w_branch_a"], t["w_branch_b"], t["w_out"]
        self.w_query, self.sub_keys = t["w_query"], t["sub_keys"]
        self.u, self.v = t["u"], t["v"]
        self.gate_mat = t["gate_mat"]
        self.out = t["out"]


def build(nc, args):
    d = Dram(args)
    m = Layer()
    place_shared(nc, m)
    project(nc, m, d)
    attend(nc, m, d)
    route(nc, m, d)
    experts(nc, m, d)


def rope_tables(np, dim):
    inv = (10000.0 ** (-np.arange(0, dim, 2) / dim)).astype(np.float32)
    ang = np.arange(KEYS, dtype=np.float32)[:, None] * inv[None, :]
    c, s = np.cos(ang.astype(np.float64)), np.sin(ang.astype(np.float64))
    out = []
    for t in (np.concatenate([c, c], 1), np.concatenate([-s, s], 1)):
        tiles = np.zeros((NT + 1, P, dim), np.float32)
        tiles[:NT] = t[META:].reshape(NT, P, dim)
        tiles[NT, :META] = t[:META]
        out.append(np.ascontiguousarray(tiles.transpose(1, 0, 2)))
    return out


def kernel(**inputs):
    import numpy as np
    import concourse.bacc as bacc
    from concourse.bass_utils import run_bass_kernel_spmd

    a = {k: np.asarray(v) for k, v in inputs.items()}

    def chunked(w):
        return np.ascontiguousarray(w.reshape(-1, P, w.shape[-1]).transpose(1, 0, 2))

    w_in = a["w_in"][0]
    names = ("aq", "ak", "av", "bq", "bk", "bv", "iq", "ik", "iw", "ga", "gb")
    widths = (512, 512, 512, 512, 64, 64, 512, 64, 8, 1024, 1024)
    cols, at = {}, 0
    for n, w in zip(names, widths):
        cols[n] = w_in[:, at:at + w]
        at += w
    wide = [cols["ak"], cols["av"], cols["aq"], cols["iq"], cols["bq"],
            cols["ga"][:, :512], cols["ga"][:, 512:], cols["gb"][:, :512], cols["gb"][:, 512:]]
    cos, sin = rope_tables(np, HEAD)
    icos, isin = rope_tables(np, IDX_ROPE)
    arrays = {
        "x": np.ascontiguousarray(a["x"][0]),
        "meta_tokens": a["meta_tokens"],
        "w_wide": np.stack([chunked(w) for w in wide]),
        "w_small": chunked(np.concatenate([cols[n] for n in ("bk", "bv", "ik", "iw")], 1)),
        "mix_gain": np.ascontiguousarray(a["mix_norm_gain"][0].reshape(DC, P).T),
        "ffn_gain": np.ascontiguousarray(a["ffn_norm_gain"][0].reshape(DC, P).T),
        "cos": cos, "sin": sin, "icos": icos, "isin": isin,
        "w_branch_a": chunked(a["w_branch_a"][0]),
        "w_branch_b": chunked(a["w_branch_b"][0]),
        "w_out": chunked(a["w_out"][0]),
        "w_query": chunked(a["peer_w_query"][0]),
        "sub_keys": np.ascontiguousarray(a["peer_sub_keys"][0].transpose(1, 3, 0, 2).reshape(P, PEER_HEADS, N_KEYS)),
        "u": np.ascontiguousarray(a["peer_u"][0].reshape(N_KEYS, N_KEYS, DC, P).transpose(1, 3, 2, 0)),
        "v": np.ascontiguousarray(a["peer_v"][0].reshape(N_KEYS, N_KEYS, D).transpose(1, 0, 2)),
    }
    for n in ("a_q_norm_gain", "a_k_norm_gain", "b_q_norm_gain", "b_k_norm_gain", "a_subln_gain",
              "a_lambda_q1", "a_lambda_k1", "a_lambda_q2", "a_lambda_k2"):
        arrays[n] = a[n][0]

    nc = bacc.Bacc("TRN2", target_bir_lowering=False, num_devices=1)
    args = {n: nc.dram_tensor("in_" + n, v.shape, mybir.dt.from_np(v.dtype), kind="ExternalInput").ap()
            for n, v in arrays.items()}
    args["out"] = nc.dram_tensor("out", (SEQ, D), F32, kind="ExternalOutput").ap()
    args["gate_mat"] = nc.dram_tensor("gate_mat", (N_KEYS, N_KEYS, SEQ), F32, kind="Internal").ap()
    build(nc, args)
    r = run_bass_kernel_spmd(nc, [{"in_" + n: v for n, v in arrays.items()}], core_ids=[0])
    return r.results[0]["out"].reshape(1, SEQ, D)
```

```python
import concourse.bass as bass
from concourse import mybir

F32 = mybir.dt.float32
F32R = mybir.dt.float32r
BF16 = mybir.dt.bfloat16
I32 = mybir.dt.int32
U32 = mybir.dt.uint32
ALU = mybir.AluOpType
ACT = mybir.ActivationFunctionType
X = mybir.AxisListType.X

P = 128
D = 1024
DC = D // P
SEQ = 512
NT = SEQ // P
META = 16
KEYS = META + SEQ
EPS = 1e-6

HEAD = 64
WIDE = 512
GROUPS = WIDE // HEAD
SMALL = 3 * HEAD + 8
A_HEADS = 4
B_HEADS = 8
IDX_HEADS = 8
IDX_ROPE = 32
TOPK = SEQ // 4
LAMBDA_INIT = 0.2

PEER_HEADS = 8
PEER_TOPK = 16
N_KEYS = 128
PEER_HALF = 64
PICKS = PEER_HEADS * PEER_TOPK
ROWS = [(a, PEER_TOPK // (a + 1)) for a in range(PEER_TOPK)]
CANDS = sum(n for _, n in ROWS)

MASKED = -1e30
UNSEEN = -1e38
TAKEN = -3e38

CHUNKS = ["ak", "small", "av", "aq", "gate", "iq", "gate", "bq", "gate", "gate"]
WITH_META = ("ak", "small", "av")
ROTATED = ("ak", "small", "aq", "iq", "bq")
STEPS = [(c, kind, i) for c, kind in enumerate(CHUNKS)
         for i in range(NT + (kind in WITH_META))]
ROT_STEPS = [n for n, (_, kind, _) in enumerate(STEPS) if kind in ROTATED]
PIECES = 2
PK = DC // PIECES
SLOTS = [(c, kind, part, i) for c, kind in enumerate(CHUNKS) for part in range(PIECES)
         for i in range(NT + (kind in WITH_META))]
EVACUATE = []
for _c, _kind, _i in STEPS:
    _at = SLOTS.index((_c, _kind, PIECES - 1, _i)) + 1 + (_i if _kind in ROTATED else 0)
    EVACUATE.append(max([_at] + EVACUATE[-1:]))
TURN = []
for _n in ROT_STEPS:
    TURN.append(max([EVACUATE[_n] + 3] + [t + 1 for t in TURN[-1:]]))
LAST_SLOT = max(TURN[-1] + 2, EVACUATE[-1] + 1)
STEP_BANKS = (0, 1, 4, 5, 6, 7)

BASE = 16896


def rows_of(i):
    return META if i == NT else P


def bcast(ap, axis, n):
    shape = list(ap.shape)
    shape.insert(axis, n)
    return ap.unsqueeze(axis).to_broadcast(shape)


class Layer:
    pass


def place_shared(nc, m):
    at = [BASE]

    def sb(name, shape, dt=F32):
        size = mybir.dt.size(dt)
        for n in shape[1:]:
            size *= n
        t = nc.alloc_sbuf_tensor_at(name, shape, dt, offset=at[0])
        at[0] += -(-size // 32) * 32
        return t

    m.stream = sb("stream", [P, NT, D])
    m.ident = sb("ident", [P, P])
    m.ident_b = sb("ident_b", [P, P], BF16)
    m.tri_b = sb("tri_b", [P, P], BF16)
    m.tri = sb("tri", [P, P])
    m.iota = sb("iota", [P, P])
    m.mix_gain = sb("mix_gain", [P, DC])
    m.ffn_gain = sb("ffn_gain", [P, DC])
    m.subln = sb("subln", [P, P])
    m.neg_lam = sb("neg_lam", [P, 1])
    m.iw = sb("iw", [P, NT, IDX_HEADS])
    m.stream_sums = sb("stream_sums", [P, NT])
    m.free0 = at[0]
    m.xh = sb("xh", [P, DC, SEQ], F32R)
    m.xl = sb("xl", [P, DC, SEQ], F32R)
    m.free1 = at[0]
    m.aqT = sb("aqT", [P, 4, SEQ])
    m.bqT = sb("bqT", [P, 4, SEQ])
    m.iqT = sb("iqT", [P, 4, SEQ])
    m.keys_at = at[0]
    m.akT = sb("akT", [P, 2, 4, KEYS])
    m.bkT = sb("bkT", [P, 2, KEYS])
    m.ikT = sb("ikT", [P, 2, KEYS])
    m.av = sb("av", [P, NT + 1, WIDE])
    m.bv = sb("bv", [P, NT + 1, HEAD])
    m.gates_at = at[0]
    m.gates = sb("gates", [P, NT, 2 * D])
    m.free2 = at[0]
    m.psum = nc.alloc_psum_tensor("psum", [P, 8 * 512], F32)


def bank(m, b, n=1):
    return m.psum[:, b * 512:(b + n) * 512]


def placer(nc, start, limit=16481 + 212860):
    at = [start]

    def sb(name, shape, dt=F32):
        size = mybir.dt.size(dt)
        for n in shape[1:]:
            size *= n
        size = -(-size // 32) * 32
        assert at[0] + size <= limit, (name, at[0] + size - limit)
        t = nc.alloc_sbuf_tensor_at(name, shape, dt, offset=at[0])
        at[0] += size
        return t
    return sb


def chain(engine, sem):
    n = [0]

    def link(ins):
        n[0] += 1
        ins.then_inc(sem, 1)
        engine.wait_ge(sem, n[0])
    return link


def inverse_root(nc, link, out, root, square):
    link(nc.vector.reciprocal(out, root))
    link(nc.vector.tensor_tensor(root, out, out, ALU.mult))
    link(nc.vector.tensor_tensor(root, root, square, ALU.mult))
    link(nc.vector.tensor_scalar(root, root, -0.5, 1.5, ALU.mult, ALU.add))
    link(nc.vector.tensor_tensor(out, out, root, ALU.mult))


def project(nc, m, d):
    wsb = placer(nc, m.free0, m.free1)
    wraw = wsb("wraw", [P, 3, PK, WIDE])
    wlo = placer(nc, m.free0)("wlo", [P, 3, PK, WIDE], F32R)
    whi = [wsb("whi0", [P, PK, WIDE], F32R)]
    sb = placer(nc, m.free2)
    xn = placer(nc, m.free2)("xn", [P, 2, D])
    whi.append(sb("whi1", [P, PK, WIDE], F32R))
    xTh = sb("xTh", [P, DC, KEYS], F32R)
    xTl = sb("xTl", [P, DC, KEYS], F32R)
    raw = sb("raw", [P, 2, WIDE])
    rot = sb("rot", [P, 2, WIDE])
    early = placer(nc, m.gates_at, m.free2)
    meta = early("meta", [META, D])
    part = sb("part", [P, 2, WIDE])
    cos = early("cos", [P, NT + 1, HEAD])
    sin = early("sin", [P, NT + 1, HEAD])
    icos = sb("icos", [P, NT + 1, IDX_ROPE])
    isin = sb("isin", [P, NT + 1, IDX_ROPE])
    gained = {k: (sb("cos_" + k, [P, NT + 1, HEAD]), sb("sin_" + k, [P, NT + 1, HEAD]))
              for k in ("aq", "ak", "bq", "bk")}
    gains = early("gains", [P, 4, HEAD])
    lams = early("lams", [P, 4, HEAD])
    lamp = early("lamp", [P, 2, HEAD])
    lam2 = sb("lam2", [P, 2])
    iota_i = early("iota_i", [P, P], I32)
    sums = sb("sums", [P, 8])
    root = sb("root", [P, 8])
    inv = sb("inv", [P, 8])
    ms = sb("ms", [P, 8])

    x_loaded = [nc.alloc_semaphore(f"x_loaded{i}") for i in range(NT + 1)]
    consts = nc.alloc_semaphore("consts")
    mix_loaded = nc.alloc_semaphore("mix_loaded")
    w_loaded = [nc.alloc_semaphore(f"w_loaded{k}") for k in range(3)]
    pool_consts = nc.alloc_semaphore("pool_consts")
    keys_zeroed = nc.alloc_semaphore("keys_zeroed")
    squared = nc.alloc_semaphore("squared")
    ms_ready = nc.alloc_semaphore("ms_ready")
    root_ready = nc.alloc_semaphore("root_ready")
    lam_dots = nc.alloc_semaphore("lam_dots")
    lam_exps = nc.alloc_semaphore("lam_exps")
    xn_ready = nc.alloc_semaphore("xn_ready")
    xn_turned = nc.alloc_semaphore("xn_turned")
    gained_x = nc.alloc_semaphore("gained_x")
    x_high = nc.alloc_semaphore("x_high")
    x_low = nc.alloc_semaphore("x_low")
    w_high = nc.alloc_semaphore("w_in_high")
    w_low = nc.alloc_semaphore("w_in_low")
    multiplied = nc.alloc_semaphore("multiplied")
    evacuated = nc.alloc_semaphore("evacuated")
    head_ms = nc.alloc_semaphore("head_ms")
    head_root = nc.alloc_semaphore("head_root")
    rotated = nc.alloc_semaphore("rotated")
    turned = nc.alloc_semaphore("turned")
    turned_out = nc.alloc_semaphore("turned_out")
    dve_order = nc.alloc_semaphore("dve_order_a")
    pool_order = nc.alloc_semaphore("pool_order_a")
    N_CONSTS = 4 + 1 + 1 + 4 + 4
    N_PIECES = PIECES * len(CHUNKS)

    def width_of(piece):
        return SMALL if CHUNKS[piece // PIECES] == "small" else WIDE

    def step_slots(n):
        c, kind, i = STEPS[n]
        return SLOTS.index((c, kind, PIECES - 1, i)) + 1

    def piece_slots(n):
        return max(k for k, (c, _, part, _) in enumerate(SLOTS) if c * PIECES + part == n) + 1

    def columns_of(i):
        return META + i * P if i < NT else 0

    def scratch_of(i):
        t = raw if i % 2 == 0 else rot
        return t[:].rearrange("p a b -> p (a b)").rearrange("p (c t) -> p c t", c=DC)[:, :, 0:rows_of(i)]

    with nc.Block() as block:
        @block.sync
        def _(sp):
            def load_weights(n):
                c, part = divmod(n, PIECES)
                w = width_of(n)
                src = d.w_small if w == SMALL else d.w_wide[c - (c > CHUNKS.index("small"))]
                sp.dma_start(wraw[:, n % 3, :, 0:w], src[:, part * PK:(part + 1) * PK]).then_inc(w_loaded[n % 3], 16)

            for i in range(NT):
                sp.dma_start(m.stream[:, i, :], d.x[i * P:(i + 1) * P, :]).then_inc(x_loaded[i], 16)
            load_weights(0)
            load_weights(1)

            def bc(row):
                return row.partition_broadcast(P)
            sp.dma_start(m.ffn_gain[:], d.ffn_gain).then_inc(consts, 16)
            for t, s in ((cos, d.cos), (sin, d.sin), (icos, d.icos), (isin, d.isin)):
                sp.dma_start(t[:], s).then_inc(consts, 16)
            sp.dma_start(m.subln[:], bc(d.a_subln_gain)).then_inc(consts, 16)
            for g, s in enumerate((d.a_q_norm_gain, d.a_k_norm_gain, d.b_q_norm_gain, d.b_k_norm_gain)):
                sp.dma_start(gains[:, g], bc(s)).then_inc(consts, 16)
            for g, s in enumerate((d.a_lambda_q1, d.a_lambda_q2, d.a_lambda_k1, d.a_lambda_k2)):
                sp.dma_start(lams[:, g], bc(s)).then_inc(consts, 16)
            for n in range(2, N_PIECES):
                if n >= 3:
                    sp.wait_ge(multiplied, piece_slots(n - 3))
                load_weights(n)

        @block.gpsimd
        def _(pool):
            link = chain(pool, pool_order)
            link(nc.gpsimd.memset(m.ident[:], 0.0))
            link(nc.gpsimd.memset(m.tri[:], 0.0))
            link(nc.gpsimd.affine_select(out=m.ident[:], in_=m.ident[:], compare_op=ALU.not_equal, fill=1.0,
                                         base=0, pattern=[[-1, P]], channel_multiplier=1))
            link(nc.gpsimd.affine_select(out=m.tri[:], in_=m.tri[:], compare_op=ALU.is_ge, fill=UNSEEN,
                                         base=0, pattern=[[-1, P]], channel_multiplier=1))
            nc.gpsimd.iota(iota_i[:], pattern=[[1, P]], base=0, channel_multiplier=0).then_inc(pool_consts, 1)
            nc.gpsimd.memset(m.akT[:], 0.0)
            nc.gpsimd.memset(m.bkT[:], 0.0)
            nc.gpsimd.memset(m.ikT[:], 0.0).then_inc(keys_zeroed, 1)
            for n in range(N_PIECES):
                w = width_of(n)
                pool.wait_ge(w_high, n + 1)
                nc.gpsimd.tensor_tensor(wlo[:, n % 3, :, 0:w], wraw[:, n % 3, :, 0:w], whi[n % 2][:, :, 0:w].bitcast(F32),
                                        ALU.subtract).then_inc(w_low, 1)

        @block.vector
        def _(dve):
            step = chain(dve, dve_order)
            step(nc.vector.memset(sums[:], 1.0))
            dve.wait_ge(pool_consts, 1)
            nc.vector.tensor_copy(m.ident_b[:], m.ident[:])
            nc.vector.tensor_scalar(m.tri_b[:], m.tri[:], MASKED / UNSEEN, None, ALU.mult)
            nc.vector.tensor_copy(m.iota[:], iota_i[:])

            dve.wait_ge(squared, NT + 1)
            nc.vector.tensor_scalar(ms[:, 0:NT + 1], sums[:, 0:NT + 1], 1.0 / D, EPS, ALU.mult, ALU.add).then_inc(ms_ready, 1)
            dve.wait_ge(root_ready, 1)
            inverse_root(nc, step, inv[:, 0:NT + 1], root[:, 0:NT + 1], ms[:, 0:NT + 1])

            def normed(i):
                r = rows_of(i)
                src = m.stream[:, i, :] if i < NT else meta[:]
                if i >= 2:
                    dve.wait_ge(xn_turned, i - 1)
                nc.vector.tensor_scalar(xn[0:r, i % 2], src, inv[0:r, i:i + 1], None, ALU.mult).then_inc(xn_ready, 1)

            def low_of(i):
                lo = columns_of(i)
                dve.wait_ge(x_high, i + 1)
                nc.vector.tensor_tensor(xTl[:, :, lo:lo + rows_of(i)], scratch_of(i),
                                        xTh[:, :, lo:lo + rows_of(i)].bitcast(F32), ALU.subtract).then_inc(x_low, 1)
            normed(0)
            normed(1)
            dve.wait_ge(mix_loaded, 16)
            for i in range(NT + 1):
                r = rows_of(i)
                dve.wait_ge(xn_turned, i + 1)
                if i >= 2:
                    dve.wait_ge(x_low, i - 1)
                ps = bank(m, 6 - 4 * (i % 2), 2).rearrange("p (c t) -> p c t", c=DC)[:, :, 0:r]
                nc.vector.tensor_tensor(scratch_of(i), ps, bcast(m.mix_gain[:], 2, r), ALU.mult).then_inc(gained_x, 1)
                if i + 2 <= NT:
                    normed(i + 2)
                dve.wait_ge(gained_x, i + 1)
                low_of(i)

            dve.wait_ge(consts, 16 * N_CONSTS)
            h = HEAD // 2
            for g, (k, scale) in enumerate((("aq", HEAD ** -0.5), ("ak", 1.0), ("bq", HEAD ** -0.5), ("bk", 1.0))):
                cg, sg = gained[k]
                if g in (0, 2):
                    step(nc.vector.tensor_scalar(gains[:, g], gains[:, g], scale, None, ALU.mult))
                nc.vector.tensor_tensor(cg[:], cos[:], bcast(gains[:, g], 1, NT + 1), ALU.mult)
                nc.vector.tensor_tensor(sg[:, :, 0:h], sin[:, :, 0:h], bcast(gains[:, g, h:], 1, NT + 1), ALU.mult)
                nc.vector.tensor_tensor(sg[:, :, h:], sin[:, :, h:], bcast(gains[:, g, 0:h], 1, NT + 1), ALU.mult)
            nc.vector.tensor_scalar(m.subln[:], m.subln[:], 1.0 - LAMBDA_INIT, None, ALU.mult)

            step(nc.vector.tensor_tensor(lamp[:], lams[:, 0:2], lams[:, 2:4], ALU.mult))
            nc.vector.tensor_reduce(lam2[:], lamp[:], X, ALU.add).then_inc(lam_dots, 1)
            dve.wait_ge(lam_exps, 1)
            step(nc.vector.tensor_tensor(m.neg_lam[:], lam2[:, 1:2], lam2[:, 0:1], ALU.subtract))
            step(nc.vector.tensor_scalar(m.neg_lam[:], m.neg_lam[:], -LAMBDA_INIT, None, ALU.add))

            def rotate(out, x, c, s, half):
                heads, r = x.shape[1], x.shape[0]
                a = part[0:r, 0, 0:heads * 2 * half].rearrange("p (h w) -> p h w", h=heads)
                b = part[0:r, 1, 0:heads * 2 * half].rearrange("p (h w) -> p h w", h=heads)
                nc.vector.tensor_tensor(a, x[:, :, 0:2 * half], bcast(c, 1, heads), ALU.mult)
                nc.vector.tensor_tensor(b[:, :, 0:half], x[:, :, half:2 * half], bcast(s[:, 0:half], 1, heads), ALU.mult)
                step(nc.vector.tensor_tensor(b[:, :, half:], x[:, :, 0:half], bcast(s[:, half:], 1, heads), ALU.mult))
                return nc.vector.tensor_tensor(out, a, b, ALU.add)

            def head_scale(x, heads, k):
                r = x.shape[0]
                sq = part[0:r, 0, 0:heads * HEAD].rearrange("p (h w) -> p h w", h=heads)
                step(nc.vector.tensor_tensor(sq, x, x, ALU.mult))
                step(nc.vector.tensor_reduce(ms[0:r, 0:heads], sq, X, ALU.add))
                nc.vector.tensor_scalar(ms[0:r, 0:heads], ms[0:r, 0:heads], 1.0 / HEAD, EPS,
                                        ALU.mult, ALU.add).then_inc(head_ms, 1)
                dve.wait_ge(head_root, k)
                inverse_root(nc, step, inv[0:r, 0:heads], root[0:r, 0:heads], ms[0:r, 0:heads])

            roots = 0
            for q, n in enumerate(ROT_STEPS):
                _, kind, i = STEPS[n]
                r = rows_of(i)
                dve.wait_ge(evacuated, n + 1)
                if q >= 1:
                    dve.wait_ge(rotated, q)
                if q >= 2:
                    dve.wait_ge(turned, q - 1)
                x = raw[0:r, q % 2]
                out = rot[0:r, q % 2]
                if kind == "small":
                    bk = x[:, 0:HEAD].rearrange("p (h w) -> p h w", h=1)
                    ik = x[:, 2 * HEAD:3 * HEAD].rearrange("p (h w) -> p h w", h=1)
                    o = out[:, 0:4 * HEAD].rearrange("p (h w) -> p h w", h=4)
                    roots += 1
                    head_scale(bk, 1, roots)
                    cg, sg = gained["bk"]
                    step(rotate(o[:, 0:1], bk, cg[0:r, i], sg[0:r, i], HEAD // 2))
                    step(nc.vector.tensor_scalar(o[:, 0], o[:, 0], inv[0:r, 0:1], None, ALU.mult))
                    step(rotate(o[:, 2:3, 0:IDX_ROPE], ik, icos[0:r, i], isin[0:r, i], IDX_ROPE // 2))
                    step(nc.vector.tensor_copy(o[:, 2, IDX_ROPE:], ik[:, 0, IDX_ROPE:]))
                    nc.vector.tensor_copy(m.bv[0:r, i], x[:, HEAD:2 * HEAD])
                    if i < NT:
                        nc.vector.tensor_scalar(m.iw[:, i], x[:, 3 * HEAD:SMALL], IDX_HEADS ** -0.5 * HEAD ** -0.5,
                                                None, ALU.mult)
                    nc.vector.tensor_copy(o[:, 1], o[:, 0])
                    nc.vector.tensor_copy(o[:, 3], o[:, 2]).then_inc(rotated, 1)
                    continue
                xh = x.rearrange("p (h w) -> p h w", h=GROUPS)
                oh = out.rearrange("p (h w) -> p h w", h=GROUPS)
                if kind == "iq":
                    nc.vector.tensor_copy(oh[:, :, IDX_ROPE:], xh[:, :, IDX_ROPE:])
                    rotate(oh[:, :, 0:IDX_ROPE], xh, icos[0:r, i], isin[0:r, i], IDX_ROPE // 2).then_inc(rotated, 1)
                    continue
                roots += 1
                head_scale(xh, GROUPS, roots)
                cg, sg = gained[kind]
                step(rotate(oh, xh, cg[0:r, i], sg[0:r, i], HEAD // 2))
                nc.vector.tensor_tensor(oh, oh, bcast(inv[0:r, 0:GROUPS], 2, HEAD), ALU.mult).then_inc(rotated, 1)

        @block.scalar
        def _(act):
            act.dma_start(meta[:], d.meta_tokens).then_inc(x_loaded[NT], 16)
            act.dma_start(m.mix_gain[:], d.mix_gain).then_inc(mix_loaded, 16)
            act.wait_ge(dve_order, 1)
            for k, i in enumerate([NT] + list(range(NT))):
                r = rows_of(i)
                act.wait_ge(x_loaded[i], 16)
                src = m.stream[:, i, :] if i < NT else meta[:]
                nc.scalar.activation(raw[0:r].rearrange("p a b -> p (a b)"), src, ACT.Square,
                                     accum_out=sums[0:r, i:i + 1]).then_inc(squared, 1)
                act.wait_ge(squared, k + 1)
            act.wait_ge(ms_ready, 1)
            nc.scalar.activation(root[:, 0:NT + 1], ms[:, 0:NT + 1], ACT.Sqrt).then_inc(root_ready, 1)

            def split_weights(n):
                act.wait_ge(w_loaded[n % 3], 16 * (n // 3 + 1))
                if n >= 2:
                    act.wait_ge(multiplied, piece_slots(n - 2))
                w = width_of(n)
                nc.scalar.copy(whi[n % 2][:, :, 0:w], wraw[:, n % 3, :, 0:w]).then_inc(w_high, 1)

            split_weights(0)
            for i in range(NT + 1):
                lo = columns_of(i)
                act.wait_ge(gained_x, i + 1)
                nc.scalar.copy(xTh[:, :, lo:lo + rows_of(i)], scratch_of(i)).then_inc(x_high, 1)
            act.wait_ge(xn_turned, NT + 1)
            split_weights(1)
            act.wait_ge(lam_dots, 1)
            nc.scalar.activation(lam2[:], lam2[:], ACT.Exp).then_inc(lam_exps, 1)

            act.wait_ge(keys_zeroed, 1)
            dests = {"aq": m.aqT, "iq": m.iqT, "bq": m.bqT}

            def turn_out(q):
                _, kind, i = STEPS[ROT_STEPS[q]]
                r = rows_of(i)
                act.wait_ge(turned, q + 1)
                ps = bank(m, 2 + q % 2).rearrange("p (c t) -> p c t", c=4)[:, :, 0:r]
                key_lo = columns_of(i)
                halves = [slice(0, HEAD), slice(HEAD, P)]
                if kind == "small":
                    for k, half in enumerate(halves):
                        nc.scalar.copy(m.bkT[half, k, key_lo:key_lo + r], ps[half, 0])
                        last = nc.scalar.copy(m.ikT[half, k, key_lo:key_lo + r], ps[half, 1])
                    last.then_inc(turned_out, 1)
                elif kind == "ak":
                    for k, half in enumerate(halves):
                        last = nc.scalar.copy(m.akT[half, k, :, key_lo:key_lo + r], ps[half])
                    last.then_inc(turned_out, 1)
                else:
                    nc.scalar.copy(dests[kind][:, :, i * P:i * P + r], ps).then_inc(turned_out, 1)

            def evacuate(n):
                c, kind, i = STEPS[n]
                r = rows_of(i)
                act.wait_ge(multiplied, step_slots(n))
                ps = bank(m, STEP_BANKS[n % 6])[0:r]
                if kind in ROTATED:
                    q = ROT_STEPS.index(n)
                    if q == 0:
                        act.wait_ge(x_low, NT + 1)
                    if q >= 2:
                        act.wait_ge(rotated, q - 1)
                    w = SMALL if kind == "small" else WIDE
                    nc.scalar.copy(raw[0:r, q % 2, 0:w], ps[:, 0:w]).then_inc(evacuated, 1)
                    if kind != "iq":
                        heads = 1 if kind == "small" else GROUPS
                        k = sum(STEPS[s][1] != "iq" for s in ROT_STEPS[:q + 1])
                        act.wait_ge(head_ms, k)
                        nc.scalar.activation(root[0:r, 0:heads], ms[0:r, 0:heads], ACT.Sqrt).then_inc(head_root, 1)
                elif kind == "av":
                    nc.scalar.copy(m.av[0:r, i], ps).then_inc(evacuated, 1)
                else:
                    g = CHUNKS[:c].count("gate")
                    nc.scalar.activation(m.gates[:, i, g * WIDE:(g + 1) * WIDE], ps, ACT.Sigmoid).then_inc(evacuated, 1)

            for slot in range(LAST_SLOT):
                if slot < len(SLOTS):
                    c, _, part, i = SLOTS[slot]
                    n = c * PIECES + part
                    if i == 0 and 1 <= n < N_PIECES - 1:
                        split_weights(n + 1)
                for n in range(len(STEPS)):
                    if EVACUATE[n] == slot:
                        evacuate(n)
                for q in range(len(TURN)):
                    if TURN[q] + 1 == slot:
                        turn_out(q)

        @block.tensor
        def _(pe):
            def turn_x(i):
                r = rows_of(i)
                pe.wait_ge(xn_ready, i + 1)
                if i >= 2:
                    pe.wait_ge(gained_x, i - 1)
                for c in range(DC):
                    last = nc.tensor.transpose(bank(m, 6 - 4 * (i % 2), 2)[:, c * P:c * P + r],
                                               xn[0:r, i % 2, c * P:(c + 1) * P], m.ident[0:r, 0:r])
                last.then_inc(xn_turned, 1)

            def turn(q):
                _, kind, i = STEPS[ROT_STEPS[q]]
                r = rows_of(i)
                pe.wait_ge(rotated, q + 1)
                if q >= 2:
                    pe.wait_ge(turned_out, q - 1)
                blocks = 2 if kind == "small" else 4
                for b in range(blocks):
                    last = nc.tensor.transpose(bank(m, 2 + q % 2)[:, b * P:b * P + r],
                                               rot[0:r, q % 2, b * P:(b + 1) * P], m.ident[0:r, 0:r])
                last.then_inc(turned, 1)

            turn_x(0)
            for slot in range(LAST_SLOT):
                if slot < NT:
                    turn_x(slot + 1)
                if slot < len(SLOTS):
                    c, kind, part, i = SLOTS[slot]
                    piece = c * PIECES + part
                    n = STEPS.index((c, kind, i))
                    if i == 0:
                        pe.wait_ge(w_low, piece + 1)
                    if slot <= NT:
                        pe.wait_ge(x_low, slot + 1)
                    if part == 0 and n >= 6:
                        pe.wait_ge(evacuated, n - 5)
                    w = width_of(piece)
                    lo = columns_of(i)
                    ps = bank(m, STEP_BANKS[n % 6])[:, 0:w]
                    for k in range(PK):
                        xh, xl = (t[:, part * PK + k, lo:lo + P] for t in (xTh, xTl))
                        wh = whi[piece % 2][:, k, 0:w]
                        wl = wlo[:, piece % 3, k, 0:w]
                        nc.tensor.matmul(ps, xh, wh, start=(part == 0 and k == 0), stop=False)
                        nc.tensor.matmul(ps, xh, wl, start=False, stop=False)
                        last = nc.tensor.matmul(ps, xl, wh, start=False, stop=(part == PIECES - 1 and k == PK - 1))
                    last.then_inc(multiplied, 1)
                for q in range(len(TURN)):
                    if TURN[q] == slot:
                        turn(q)


UNITS = A_HEADS + B_HEADS
ALL_UNITS = [(i, kind, h) for i in range(NT)
             for kind, heads in (("a", A_HEADS), ("b", B_HEADS)) for h in range(heads)]
ROUNDS = TOPK // 8
IDX_PER_UNIT = IDX_HEADS // A_HEADS
LATE_ROUNDS = [ROUNDS // A_HEADS] + [1] * (NT - 2) + [2]


def early_rounds(i, h):
    n = ROUNDS - A_HEADS * LATE_ROUNDS[i]
    return n * h // B_HEADS, n * (h + 1) // B_HEADS




def keys_of(i):
    return META + (i + 1) * P


def blocks_of(i):
    return [(META + b * P, P, b, b * P) for b in range(i + 1)] + [(0, META, NT, NT * P)]


def scores_of_unit(i, kind, h):
    return [(i, kind, h, s) for s in range(2 if kind == "a" else 1)]


def scores_beside(i, kind, h):
    heads = range(IDX_PER_UNIT * h, IDX_PER_UNIT * (h + 1)) if kind == "a" and i + 1 < NT else ()
    return [(i + 1, "idx", head, 0) for head in heads]


PLAN = [(0, "idx", h, 0) for h in range(IDX_HEADS)] + [s for u in ALL_UNITS for s in scores_of_unit(*u) + scores_beside(*u)]
SCORE = {key: n for n, key in enumerate(PLAN)}


def score_banks():
    out, users, at = [], {}, 0
    for n, (i, _, _, _) in enumerate(PLAN):
        wide = 1 + (keys_of(i) > 512)
        at += at % wide
        mine = [(at + b) % 4 for b in range(wide)]
        out.append((mine[0], max(users.get(b, -1) for b in mine)))
        users.update({b: n for b in mine})
        at += wide
    return out


SCORE_BANKS = score_banks()


def probs_slot(kind, h, s):
    return 2 * (h % 2) + s if kind == "a" else h % 4


def probs_users():
    out, users = {}, {}
    for u, (i, kind, h) in enumerate(ALL_UNITS):
        for s in range(2 if kind == "a" else 1):
            slot = probs_slot(kind, h, s)
            out[(i, kind, h, s)] = users.get(slot, -1)
            users[slot] = u
    return out


PROBS_USERS = probs_users()


def softmaxes_before(i, kind, h, s=0):
    return i * (2 * A_HEADS + B_HEADS) + (2 * h + s if kind == "a" else 2 * A_HEADS + h)


def attend(nc, m, d):
    w_out = placer(nc, m.free0, m.free1)("w_out", [P, DC, D])
    late = placer(nc, m.free1, m.free1 + 4 * 3 * 4 * SEQ)
    outT = late("outT", [P, 2, 8, P])
    mixed = late("mixed", [P, D])
    mixedT = late("mixedT", [P, DC, P])
    sq = late("sq_s", [P, WIDE])
    squares = late("squares", [P, D])
    sb = placer(nc, m.free2)
    w_a = placer(nc, m.keys_at, m.keys_at + 4 * 2 * 4 * KEYS)("w_a", [P, 4, D])
    w_b = sb("w_b", [P, 4, D])
    probs = sb("probs", [P, 4, KEYS])
    pT = sb("pT", [P, 2, (NT + 1) * P])
    score = sb("score", [P, 2, KEYS])
    bias = sb("bias", [P, 2, KEYS], BF16)
    relu_ring = sb("relu_ring", [P, 4, KEYS])
    out_a = sb("out_a", [P, NT, WIDE])
    out_b = sb("out_b", [P, NT, WIDE])
    maxima = sb("maxima", [P, ROUNDS, 8])
    nmax = sb("nmax", [P, 16])
    total = sb("total", [P, 16])
    ratio = sb("ratio", [P, A_HEADS])
    recip = sb("recip", [P, 12])
    ms = sb("ms_s", [P, A_HEADS])
    root = sb("root_s", [P, A_HEADS])
    inv = sb("inv_s", [P, A_HEADS])

    weights = nc.alloc_semaphore("weights_b")
    scored = nc.alloc_semaphore("scored")
    scores_used = nc.alloc_semaphore("scores_used")
    max_ready = nc.alloc_semaphore("max_ready")
    idx_added = nc.alloc_semaphore("idx_added")
    bias_ready = nc.alloc_semaphore("bias_ready")
    combined = nc.alloc_semaphore("combined")
    p_turned = nc.alloc_semaphore("p_turned")
    pT_ready = nc.alloc_semaphore("pT_ready")
    valued = nc.alloc_semaphore("valued")
    a_read = nc.alloc_semaphore("a_read")
    b_read = nc.alloc_semaphore("b_read")
    sub_ms = nc.alloc_semaphore("sub_ms")
    sub_root = nc.alloc_semaphore("sub_root")
    outs_ready = nc.alloc_semaphore("outs_ready")
    outs_turned = nc.alloc_semaphore("outs_turned")
    outT_ready = nc.alloc_semaphore("outT_ready")
    branched = nc.alloc_semaphore("branched")
    mixed_ready = nc.alloc_semaphore("mixed_ready")
    mixed_turned = nc.alloc_semaphore("mixed_turned")
    mixedT_ready = nc.alloc_semaphore("mixedT_ready")
    outed = nc.alloc_semaphore("outed")
    streamed = nc.alloc_semaphore("streamed")
    squared_b = nc.alloc_semaphore("squared_b")
    dve_order = nc.alloc_semaphore("dve_order_b")

    def unit(i, kind, h):
        return i * UNITS + (h if kind == "a" else A_HEADS + h)

    def score_bank(n):
        i = PLAN[n][0]
        return bank(m, SCORE_BANKS[n][0], 1 + (keys_of(i) > 512))[:, 0:keys_of(i)]

    with nc.Block() as block:
        @block.sync
        def _(sp):
            sp.dma_start(w_b[:], d.w_branch_b).then_inc(weights, 16)
            sp.dma_start(w_out[:], d.w_out).then_inc(weights, 16)
            sp.wait_ge(scored, SCORE[(NT - 1, "a", A_HEADS - 1, 1)] + 1)
            sp.dma_start(w_a[:], d.w_branch_a).then_inc(weights, 16)

        @block.tensor
        def _(pe):
            def score_of(i, kind, h, s):
                n = SCORE[(i, kind, h, s)]
                w = keys_of(i)
                before = SCORE_BANKS[n][1]
                if before >= 0:
                    pe.wait_ge(scores_used, before + 1)
                if kind == "idx":
                    block_, q, k = h // 2, m.iqT, m.ikT[:, h % 2]
                elif kind == "a":
                    block_, q, k = h, m.aqT, m.akT[:, s, h]
                else:
                    block_, q, k = h // 2, m.bqT, m.bkT[:, h % 2]
                    pe.wait_ge(bias_ready, i + 1)
                ps = score_bank(n)
                for c in range(0, w, 512):
                    e = min(w, c + 512)
                    plain = kind == "idx"
                    last = nc.tensor.matmul(ps[:, c:e], q[:, block_, i * P:(i + 1) * P], k[:, c:e],
                                            start=True, stop=plain, skip_group_check=True)
                    if kind == "b":
                        last = nc.tensor.matmul(ps[:, c:e], m.ident_b[:], bias[:, i % 2, c:e], start=False, stop=True,
                                                skip_group_check=True)
                if kind == "a":
                    for c in range(0, w, 512):
                        f, e = max(c, w - P), min(w, c + 512)
                        if f < e:
                            last = nc.tensor.matmul(ps[:, f:e], m.ident_b[:], m.tri_b[:, f - (w - P):e - (w - P)],
                                                    start=False, stop=True, skip_group_check=True)
                last.then_inc(scored, 1)

            def turn(i, kind, h):
                u = unit(i, kind, h)
                if kind == "a":
                    pe.wait_ge(combined, i * A_HEADS + h + 1)
                    p = probs[:, 2 * (h % 2)]
                else:
                    pe.wait_ge(scores_used, SCORE[(i, "b", h, 0)] + 1)
                    p = probs[:, h % 4]
                if u >= 1:
                    pe.wait_ge(pT_ready, u)
                for key, n, _, col in blocks_of(i):
                    last = nc.tensor.transpose(bank(m, 4, 2)[0:n, col:col + P], p[:, key:key + n], m.ident[:])
                last.then_inc(p_turned, 1)

            def value(i, kind, h):
                u = unit(i, kind, h)
                pe.wait_ge(pT_ready, u + 1)
                if h == 0 and i >= 1:
                    pe.wait_ge(a_read if kind == "a" else b_read, i)
                blocks = blocks_of(i)
                for k, (_, n, t, col) in enumerate(blocks):
                    if kind == "a":
                        dst, v = bank(m, 6)[:, h * P:(h + 1) * P], m.av[0:n, t, h * P:(h + 1) * P]
                    else:
                        dst, v = bank(m, 7)[:, h * HEAD:(h + 1) * HEAD], m.bv[0:n, t]
                    last = nc.tensor.matmul(dst, pT[0:n, u % 2, col:col + P], v,
                                            start=(k == 0), stop=(k == len(blocks) - 1), skip_group_check=True)
                last.then_inc(valued, 1)

            for h in range(IDX_HEADS):
                score_of(0, "idx", h, 0)
            for k in range(len(ALL_UNITS) + 3):
                if k < len(ALL_UNITS):
                    for key in scores_of_unit(*ALL_UNITS[k]):
                        score_of(*key)
                if k >= 3:
                    value(*ALL_UNITS[k - 3])
                if 2 <= k < len(ALL_UNITS) + 2:
                    turn(*ALL_UNITS[k - 2])
                if k < len(ALL_UNITS):
                    for key in scores_beside(*ALL_UNITS[k]):
                        score_of(*key)

            def turn_outs(i):
                if i >= 2:
                    pe.wait_ge(mixedT_ready, i - 1)
                pe.wait_ge(outs_ready, i + 1)
                for br, src in ((1, out_b), (0, out_a)):
                    for c in range(4):
                        last = nc.tensor.transpose(bank(m, 4 + br)[:, c * P:(c + 1) * P],
                                                   src[:, i, c * P:(c + 1) * P], m.ident[:])
                    last.then_inc(outs_turned, 1)

            def branch(i):
                if i >= 1:
                    pe.wait_ge(mixed_ready, i)
                for k, (br, w) in enumerate(((1, w_b), (0, w_a))):
                    pe.wait_ge(outT_ready, 2 * i + k + 1)
                    for half in range(2):
                        for c in range(4):
                            last = nc.tensor.matmul(bank(m, 2 * br + half), outT[:, i % 2, 4 * br + c, :],
                                                    w[:, c, half * 512:(half + 1) * 512],
                                                    start=(c == 0), stop=(c == 3))
                    last.then_inc(branched, 1)

            def turn_mixed(i):
                pe.wait_ge(mixed_ready, i + 1)
                pe.wait_ge(outT_ready, 2 * min(i + 2, NT))
                for c in range(DC):
                    last = nc.tensor.transpose(bank(m, 4, 2)[:, c * P:(c + 1) * P], mixed[:, c * P:(c + 1) * P],
                                               m.ident[:])
                last.then_inc(mixed_turned, 1)

            def output(i):
                pe.wait_ge(mixedT_ready, i + 1)
                if i >= 1:
                    pe.wait_ge(streamed, i)
                for half in range(2):
                    for c in range(DC):
                        last = nc.tensor.matmul(bank(m, 6 + half), mixedT[:, c, :],
                                                w_out[:, c, half * 512:(half + 1) * 512],
                                                start=(c == 0), stop=(c == DC - 1))
                last.then_inc(outed, 1)

            pe.wait_ge(weights, 48)
            pe.wait_ge(a_read, NT)
            pe.wait_ge(b_read, NT)
            turn_outs(0)
            for i in range(NT + 1):
                if i < NT:
                    branch(i)
                if i >= 1:
                    output(i - 1)
                if i + 1 < NT:
                    turn_outs(i + 1)
                if i < NT:
                    turn_mixed(i)

        @block.scalar
        def _(act):
            def turn_out(i, kind, h):
                u = unit(i, kind, h)
                act.wait_ge(p_turned, u + 1)
                if u >= 2:
                    act.wait_ge(valued, u - 1)
                nc.scalar.copy(pT[:, u % 2, 0:(i + 1) * P], bank(m, 4)[:, 0:(i + 1) * P])
                nc.scalar.copy(pT[0:META, u % 2, NT * P:], bank(m, 5)[0:META, 0:P]).then_inc(pT_ready, 1)

            def use_score(i, kind, h, s):
                n = SCORE[(i, kind, h, s)]
                w = keys_of(i)
                if kind == "idx":
                    act.wait_ge(scored, n + 1)
                    if i * IDX_HEADS + h >= 4:
                        act.wait_ge(idx_added, i * IDX_HEADS + h - 3)
                    nc.scalar.activation(relu_ring[:, h % 4, 0:w], score_bank(n), ACT.Relu).then_inc(scores_used, 1)
                    return
                j = softmaxes_before(i, kind, h, s)
                act.wait_ge(max_ready, j + 1)
                before = PROBS_USERS[(i, kind, h, s)]
                if before >= 0:
                    act.wait_ge(p_turned, before + 1)
                slot = probs_slot(kind, h, s)
                jj = j % 16
                nc.scalar.activation(probs[:, slot, 0:w], score_bank(n), ACT.Exp,
                                     bias=nmax[:, jj:jj + 1], accum_out=total[:, jj:jj + 1]).then_inc(scores_used, 1)

            for h in range(IDX_HEADS):
                use_score(0, "idx", h, 0)
            for k in range(len(ALL_UNITS) + 2):
                if k < len(ALL_UNITS):
                    for key in scores_of_unit(*ALL_UNITS[k]):
                        use_score(*key)
                if k >= 2:
                    turn_out(*ALL_UNITS[k - 2])
                if k < len(ALL_UNITS):
                    for key in scores_beside(*ALL_UNITS[k]):
                        use_score(*key)

            def sub_norm(i):
                act.wait_ge(sub_ms, i + 1)
                nc.scalar.activation(root[:], ms[:], ACT.Sqrt).then_inc(sub_root, 1)

            def outs_out(i):
                for k, br in enumerate((1, 0)):
                    act.wait_ge(outs_turned, 2 * i + k + 1)
                    if i >= 2:
                        act.wait_ge(branched, 2 * i - 2)
                    nc.scalar.copy(outT[:, i % 2, 4 * br:4 * br + 4, :].rearrange("p c t -> p (c t)"),
                                   bank(m, 4 + br)).then_inc(outT_ready, 1)

            def mixed_out(i):
                act.wait_ge(mixed_turned, i + 1)
                if i >= 1:
                    act.wait_ge(outed, i)
                nc.scalar.copy(mixedT[:].rearrange("p c t -> p (c t)"), bank(m, 4, 2)).then_inc(mixedT_ready, 1)

            def squares_of(i):
                act.wait_ge(streamed, i + 1)
                if i >= 1:
                    act.wait_ge(squared_b, i)
                nc.scalar.activation(squares[:], m.stream[:, i, :], ACT.Square,
                                     accum_out=m.stream_sums[:, i:i + 1]).then_inc(squared_b, 1)

            sub_norm(0)
            outs_out(0)
            sub_norm(1)
            for i in range(NT):
                if i + 1 < NT:
                    outs_out(i + 1)
                if i + 2 < NT:
                    sub_norm(i + 2)
                mixed_out(i)
                if i >= 2:
                    squares_of(i - 2)
            squares_of(NT - 2)
            squares_of(NT - 1)

        @block.vector
        def _(dve):
            link = chain(dve, dve_order)

            def rounds(i, first, n):
                w = keys_of(i)
                for r in range(first, first + n):
                    link(nc.vector.max(maxima[:, r], score[:, i % 2, 0:w]))
                    link(nc.vector.match_replace(score[:, i % 2, 0:w], maxima[:, r], score[:, i % 2, 0:w], TAKEN))

            def add_index(i, h):
                w = keys_of(i)
                dve.wait_ge(scores_used, SCORE[(i, "idx", h, 0)] + 1)
                r, out = relu_ring[:, h % 4, 0:w], score[:, i % 2, 0:w]
                if h == 0:
                    ins = nc.vector.tensor_scalar(out, r, m.iw[:, i, 0:1], None, ALU.mult)
                else:
                    ins = nc.vector.scalar_tensor_tensor(out, r, m.iw[:, i, h:h + 1], out, ALU.mult, ALU.add)
                ins.then_inc(idx_added, 1)
                dve.wait_ge(idx_added, i * IDX_HEADS + h + 1)
                if h == IDX_HEADS - 1:
                    link(nc.vector.tensor_tensor(out[:, w - P:w], out[:, w - P:w], m.tri[:], ALU.add))

            def mask(i):
                w = keys_of(i)
                out = score[:, i % 2, 0:w]
                link(nc.vector.tensor_scalar(out, out, 2 * UNSEEN, MASKED, ALU.is_gt, ALU.mult))
                link(nc.vector.tensor_tensor(out[:, w - P:w], out[:, w - P:w], m.tri_b[:], ALU.add))
                nc.vector.tensor_copy(bias[:, i % 2, 0:w], out).then_inc(bias_ready, 1)

            def max_of(i, kind, h, s):
                n = SCORE[(i, kind, h, s)]
                jj = softmaxes_before(i, kind, h, s) % 16
                dve.wait_ge(scored, n + 1)
                nc.vector.tensor_reduce(nmax[:, jj:jj + 1], score_bank(n), X, ALU.max,
                                        negate=True).then_inc(max_ready, 1)

            def combine(i, h):
                w = keys_of(i)
                dve.wait_ge(scores_used, SCORE[(i, "a", h, 1)] + 1)
                nc.vector.reciprocal(recip[:, h:h + 1], total[:, 2 * h:2 * h + 1])
                link(nc.vector.reciprocal(ratio[:, h:h + 1], total[:, 2 * h + 1:2 * h + 2]))
                link(nc.vector.tensor_scalar(ratio[:, h:h + 1], ratio[:, h:h + 1], total[:, 2 * h:2 * h + 1],
                                             m.neg_lam[:, 0:1], ALU.mult, ALU.mult))
                s0 = 2 * (h % 2)
                nc.vector.scalar_tensor_tensor(probs[:, s0, 0:w], probs[:, s0 + 1, 0:w], ratio[:, h:h + 1],
                                               probs[:, s0, 0:w], ALU.mult, ALU.add).then_inc(combined, 1)

            def read_a(i):
                dve.wait_ge(valued, unit(i, "a", A_HEADS - 1) + 1)
                nc.vector.tensor_tensor(out_a[:, i].rearrange("p (h w) -> p h w", h=A_HEADS),
                                        bank(m, 6).rearrange("p (h w) -> p h w", h=A_HEADS),
                                        bcast(recip[:, 0:A_HEADS], 2, P), ALU.mult).then_inc(a_read, 1)

            def read_b(i):
                dve.wait_ge(scores_used, SCORE[(i, "b", B_HEADS - 1, 0)] + 1)
                link(nc.vector.reciprocal(recip[:, A_HEADS:], total[:, 2 * A_HEADS:]))
                dve.wait_ge(valued, unit(i, "b", B_HEADS - 1) + 1)
                nc.vector.tensor_tensor(out_b[:, i].rearrange("p (h w) -> p h w", h=B_HEADS),
                                        bank(m, 7).rearrange("p (h w) -> p h w", h=B_HEADS),
                                        bcast(recip[:, A_HEADS:], 2, HEAD), ALU.mult).then_inc(b_read, 1)

            for h in range(IDX_HEADS):
                add_index(0, h)
            for i in range(NT):
                for h in range(A_HEADS):
                    max_of(i, "a", h, 0)
                    max_of(i, "a", h, 1)
                    late = LATE_ROUNDS[i]
                    rounds(i, ROUNDS - (A_HEADS - h) * late, late)
                    if h >= 1 and i + 1 < NT:
                        for s in range(IDX_PER_UNIT):
                            add_index(i + 1, (h - 1) * IDX_PER_UNIT + s)
                    combine(i, h)
                mask(i)
                if i >= 1:
                    read_b(i - 1)
                for h in range(B_HEADS):
                    max_of(i, "b", h, 0)
                    if h == 3:
                        read_a(i)
                    if i + 1 < NT:
                        if h == 0:
                            for s in range(IDX_PER_UNIT):
                                add_index(i + 1, (A_HEADS - 1) * IDX_PER_UNIT + s)
                        first, last = early_rounds(i + 1, h)
                        rounds(i + 1, first, last - first)
            read_b(NT - 1)
            dve.wait_ge(a_read, NT)
            dve.wait_ge(b_read, NT)

            def sub_norm(i):
                a = out_a[:, i]
                link(nc.vector.tensor_tensor(sq[:], a, a, ALU.mult))
                link(nc.vector.tensor_reduce(ms[:], sq[:].rearrange("p (h w) -> p h w", h=A_HEADS), X, ALU.add))
                nc.vector.tensor_scalar(ms[:], ms[:], 1.0 / P, EPS, ALU.mult, ALU.add).then_inc(sub_ms, 1)
                dve.wait_ge(sub_root, i + 1)
                inverse_root(nc, link, inv[:], root[:], ms[:])
                a3 = a.rearrange("p (h w) -> p h w", h=A_HEADS)
                link(nc.vector.tensor_tensor(a3, a3, bcast(inv[:], 2, P), ALU.mult))
                nc.vector.tensor_tensor(a3, a3, bcast(m.subln[:], 1, A_HEADS), ALU.mult).then_inc(outs_ready, 1)

            def mix(i):
                ga, gb = m.gates[:, i, 0:D], m.gates[:, i, D:]
                dve.wait_ge(branched, 2 * i + 1)
                link(nc.vector.tensor_tensor(gb, gb, bank(m, 2, 2), ALU.mult))
                dve.wait_ge(branched, 2 * i + 2)
                link(nc.vector.tensor_tensor(ga, ga, bank(m, 0, 2), ALU.mult))
                if i >= 1:
                    dve.wait_ge(mixed_turned, i)
                nc.vector.tensor_tensor(mixed[:], ga, gb, ALU.add).then_inc(mixed_ready, 1)

            def residual(i):
                dve.wait_ge(outed, i + 1)
                nc.vector.tensor_tensor(m.stream[:, i, :], m.stream[:, i, :], bank(m, 6, 2),
                                        ALU.add).then_inc(streamed, 1)

            sub_norm(0)
            sub_norm(1)
            for i in range(NT):
                mix(i)
                if i + 2 < NT:
                    sub_norm(i + 2)
                if i >= 1:
                    residual(i - 1)
            residual(NT - 1)


HOT = 4
TURN_TOKENS = 8 * HOT
TURNS = P // TURN_TOKENS
TURN_GROUPS = TURN_TOKENS // HOT
COLUMN_GROUPS = TURN_GROUPS // 2
STORES = 8
TAIL = STORES
AHEAD = (N_KEYS // 2 - TAIL) // NT - TURNS
PAIRS_OF_TILE = AHEAD + TURNS
HIT_HEADS = 2
assert AHEAD > STORES
assert PAIRS_OF_TILE * NT + TAIL == N_KEYS // 2 and COLUMN_GROUPS % 2 == 0


def route(nc, m, d):
    sb = placer(nc, m.free1)
    stage = sb("stage", [P, N_KEYS, P])
    early = placer(nc, m.free1, m.free1 + 4 * N_KEYS * P)
    wq = early("wq", [P, DC, D])
    hn = early("hn", [P, 2, D])
    hnT = early("hnT", [P, 2, DC, P])
    q_sb = early("q_sb", [P, D])
    u = sb("u", [P, 2, DC, P])
    uh = sb("uh", [P, 2, DC, P], F32R)
    ul = sb("ul", [P, 2, DC, P], F32R)
    act_w = sb("act_w", [P, 2, SEQ])
    keysT = sb("keysT", [P, 2, PEER_HEADS, N_KEYS])
    qT = sb("qT", [P, NT, PEER_HEADS, P])
    s_sb = sb("s_sb", [P, 2 * PEER_HEADS, N_KEYS])
    root = sb("root_r", [P, NT])
    ms = sb("ms_r", [P, NT])
    inv = sb("inv_r", [P, NT])
    val = sb("val", [P, 2 * PEER_HEADS, PEER_TOPK])
    idx = sb("idx", [P, 2 * PEER_HEADS, PEER_TOPK], U32)
    idx_f = sb("idx_f", [P, 2 * PEER_HEADS, PEER_TOPK])
    cand = sb("cand", [P, PEER_HEADS, CANDS])
    code = sb("code", [P, PEER_HEADS, CANDS])
    top = sb("top", [P, PEER_HEADS, PEER_TOPK])
    top_at = sb("top_at", [P, PEER_HEADS, PEER_TOPK], U32)
    top_at_f = sb("top_at_f", [P, PEER_HEADS, PEER_TOPK])
    hits = sb("hits", [P, HIT_HEADS, PEER_TOPK, CANDS])
    pick = sb("pick", [P, PEER_HEADS, PEER_TOPK])
    pick_i = sb("pick_i", [P, 3, PICKS], I32)
    picks = sb("picks", [P, 3, PICKS])
    norm = sb("norm", [P, PEER_HEADS])
    picksT = sb("picksT", [P, 2, 3, P])
    hot_i = sb("hot_i", [P, 2, HOT, N_KEYS])
    hot_j = sb("hot_j", [P, 2, HOT, N_KEYS])

    wq_loaded = [nc.alloc_semaphore(f"wq_loaded{k}") for k in range(2)]
    names = ("keys_loaded ms_ready_c root_ready_c hn_ready hn_turned hnT_ready queried q_out q_turned "
             "qT_ready routed s_out s_read shifted exped picks_ready picks_turned picksT_ready "
             "x_split hot_ready hot_used gate_out stage_stored u_high u_low hidden activated dve_order_c").split()
    s = {n: nc.alloc_semaphore(n) for n in names}
    u_loaded = [nc.alloc_semaphore(f"u_loaded{k}") for k in range(2)]
    act_stored = [nc.alloc_semaphore(f"act_stored{k}") for k in range(2)]

    m.route_stores = [(act_stored[0], 16 * N_KEYS // 2), (act_stored[1], 16 * N_KEYS // 2),
                      (s["stage_stored"], 16 * NT * STORES)]

    def ahead(engine, i, body):
        at = i * PAIRS_OF_TILE
        if i == 0:
            body(0, True, False)
        with engine.Fori(int(i == 0), AHEAD - 1) as p:
            body(p + at, False, False)

    def bridge(i, body):
        body(i * PAIRS_OF_TILE + AHEAD - 1, False, False)

    def turns(engine, i, body):
        with engine.Fori(0, TURNS) as t:
            body(t, t + (i * PAIRS_OF_TILE + AHEAD))

    def tail(engine, body):
        with engine.Fori(NT * PAIRS_OF_TILE, N_KEYS // 2 - 1) as p:
            body(p, False, False)
        body(N_KEYS // 2 - 1, False, True)

    with nc.Block() as block:
        @block.sync
        def _(sp):
            def load(n, k):
                sp.dma_start(u[:, k], d.u[bass.ds(n, 1)].rearrange("o p c i -> (o p) c i")).then_inc(u_loaded[k], 16)

            def columns(pair, last):
                for k in range(2):
                    n = pair * 2 + k
                    if not last:
                        sp.wait_ge(s["u_low"], n + 1)
                        load(n + 2, k)
                    sp.wait_ge(s["activated"], n + 1)
                    sp.dma_start(d.act_mat[bass.ds(n, 1)].rearrange("o i t -> (o i) t"), act_w[:, k]
                                 ).then_inc(act_stored[k], 16)

            for half in range(2):
                cols = slice(half * 512, (half + 1) * 512)
                sp.dma_start(wq[:, :, cols], d.w_query[:, :, cols]).then_inc(wq_loaded[half], 16)
            sp.dma_start(keysT[:], d.sub_keys).then_inc(s["keys_loaded"], 16)
            load(0, 0)
            load(1, 1)
            def store_gates(i, part):
                w = N_KEYS // STORES
                sp.dma_start(d.gate_mat[bass.ds(part * w, w), :, i * P:(i + 1) * P].rearrange("j i t -> i j t"),
                             stage[:, bass.ds(part * w, w), :]).then_inc(s["stage_stored"], 16)

            def with_stores(i, pair, pairs, last=False):
                sp.wait_ge(s["gate_out"], 2 + (i + 1) * P // HOT)
                with sp.Fori(0, STORES - int(last)) as part:
                    store_gates(i, part)
                    columns(part + pair, False)
                if last:
                    store_gates(i, STORES - 1)
                    columns(pair + STORES - 1, True)
                elif pairs > STORES:
                    with sp.Fori(pair + STORES, pair + pairs) as p:
                        columns(p, False)

            for i in range(NT):
                if i == 0:
                    ahead(sp, i, lambda pair, first, last: columns(pair, last))
                else:
                    with_stores(i - 1, i * PAIRS_OF_TILE, AHEAD - 1)
                bridge(i, lambda pair, first, last: columns(pair, last))
                turns(sp, i, lambda t, pair: columns(pair, False))
            with_stores(NT - 1, NT * PAIRS_OF_TILE, TAIL, last=True)

        @block.tensor
        def _(pe):
            pe.sem_inc(s["hot_used"], 2)

            def query(i):
                pe.wait_ge(s["hn_ready"], i + 1)
                if i >= 1:
                    pe.wait_ge(s["hnT_ready"], i)
                for c in range(DC):
                    last = nc.tensor.transpose(bank(m, 0, 2)[:, c * P:(c + 1) * P], hn[:, i % 2, c * P:(c + 1) * P],
                                               m.ident[:])
                last.then_inc(s["hn_turned"], 1)
                pe.wait_ge(s["hnT_ready"], i + 1)
                if i >= 1:
                    pe.wait_ge(s["q_out"], i)
                for half in range(2):
                    if i == 0:
                        pe.wait_ge(wq_loaded[half], 16)
                    for c in range(DC):
                        last = nc.tensor.matmul(bank(m, 2 + half), hnT[:, i % 2, c, :],
                                                wq[:, c, half * 512:(half + 1) * 512],
                                                start=(c == 0), stop=(c == DC - 1))
                last.then_inc(s["queried"], 1)

            def turn_query(i):
                pe.wait_ge(s["q_out"], i + 1)
                if i >= 1:
                    pe.wait_ge(s["qT_ready"], i)
                for h in range(PEER_HEADS):
                    last = nc.tensor.transpose(bank(m, 4, 2)[:, h * P:(h + 1) * P], q_sb[:, h * P:(h + 1) * P], m.ident[:])
                last.then_inc(s["q_turned"], 1)

            def score(i):
                if i == 0:
                    pe.wait_ge(s["keys_loaded"], 16)
                    pe.wait_ge(s["qT_ready"], NT)
                    pe.wait_ge(s["hnT_ready"], NT)
                    pe.wait_ge(s["q_out"], NT)
                for h in range(PEER_HEADS):
                    for c in range(2):
                        last = nc.tensor.matmul(bank(m, 2 * c, 2)[:, h * P:(h + 1) * P],
                                                qT[:, i, h, :], keysT[:, c, h, :],
                                                start=True, stop=True, skip_group_check=True)
                last.then_inc(s["routed"], 1)

            def column(n, k, first, lo=0, hi=DC):
                if lo == 0:
                    pe.wait_ge(s["u_low"], n + 1)
                    if not first:
                        pe.wait_ge(s["activated"], n - 1)
                for c in range(lo, hi):
                    nc.tensor.matmul(bank(m, 4 + k), uh[:, k, c], m.xh[:, c], start=(c == 0), stop=False)
                    nc.tensor.matmul(bank(m, 4 + k), uh[:, k, c], m.xl[:, c], start=False, stop=False)
                    last = nc.tensor.matmul(bank(m, 4 + k), ul[:, k, c], m.xh[:, c], start=False, stop=(c == DC - 1))
                if hi == DC:
                    last.then_inc(s["hidden"], 1)

            def alone(pair, first, last):
                for k in range(2):
                    column(pair * 2 + k, k, first)

            def gates(i):
                def body(t, pair):
                    for g in range(TURN_GROUPS):
                        b = g % 2
                        n = t * TURN_GROUPS + (i * TURNS * TURN_GROUPS + g + 1)
                        pe.wait_ge(s["hot_ready"], n)
                        pe.wait_ge(s["gate_out"], n)
                        for q in range(HOT):
                            last_mm = nc.tensor.matmul(bank(m, 6 + b)[:, q * P:(q + 1) * P], hot_i[:, b, q],
                                                       hot_j[:, b, q], start=True, stop=True, skip_group_check=True)
                        last_mm.then_inc(s["hot_used"], 1)
                        if b == 1:
                            k = g // COLUMN_GROUPS
                            at = g % COLUMN_GROUPS + 1
                            column(pair * 2 + k, k, False, (at - 2) * DC // COLUMN_GROUPS, at * DC // COLUMN_GROUPS)
                turns(pe, i, body)

            for i in range(NT):
                query(i)
                if i >= 1:
                    turn_query(i - 1)
            turn_query(NT - 1)
            score(0)
            pe.wait_ge(s["x_split"], NT)
            for i in range(NT):
                ahead(pe, i, alone)
                bridge(i, alone)
                pe.wait_ge(s["picks_ready"], i + 1)
                if i >= 1:
                    pe.wait_ge(s["gate_out"], 2 + i * P // HOT)
                for k in range(3):
                    last = nc.tensor.transpose(bank(m, 7)[:, k * P:(k + 1) * P], picks[:, k], m.ident[:])
                last.then_inc(s["picks_turned"], 1)
                if i + 1 < NT:
                    pe.wait_ge(s["s_out"], i + 1)
                    score(i + 1)
                pe.wait_ge(s["picksT_ready"], i + 1)
                gates(i)
            tail(pe, alone)

        @block.scalar
        def _(act):
            act.sem_inc(s["gate_out"], 2)

            def u_high(n, k):
                act.wait_ge(u_loaded[k], (n - k) * 8 + 16)
                nc.scalar.copy(uh[:, k], u[:, k]).then_inc(s["u_high"], 1)

            def column(n, k, pair, first, last):
                act.wait_ge(s["hidden"], n + 1)
                if not first:
                    act.wait_ge(act_stored[k], pair * 16)
                nc.scalar.activation(act_w[:, k], bank(m, 4 + k), ACT.Gelu).then_inc(s["activated"], 1)
                if not last:
                    u_high(n + 2, k)

            def alone(pair, first, last):
                for k in range(2):
                    column(pair * 2 + k, k, pair, first, last)

            def query_out(i):
                act.wait_ge(s["queried"], i + 1)
                if i >= 1:
                    act.wait_ge(s["q_turned"], i)
                nc.scalar.copy(q_sb[:], bank(m, 2, 2)).then_inc(s["q_out"], 1)

            def query_turned(i):
                act.wait_ge(s["q_turned"], i + 1)
                nc.scalar.copy(qT[:, i].rearrange("p h t -> p (h t)"), bank(m, 4, 2)).then_inc(s["qT_ready"], 1)

            def score_out(i):
                act.wait_ge(s["routed"], i + 1)
                if i >= 1:
                    act.wait_ge(s["s_read"], i)
                nc.scalar.copy(s_sb[:].rearrange("p h k -> p (h k)"), bank(m, 0, 4)).then_inc(s["s_out"], 1)

            def gates(i):
                if i >= 1:
                    act.wait_ge(s["stage_stored"], 16 * i * STORES)

                def body(t, pair):
                    for g in range(TURN_GROUPS):
                        b = g % 2
                        act.wait_ge(s["hot_used"], t * TURN_GROUPS + (i * TURNS * TURN_GROUPS + g + 3))
                        at = t * TURN_TOKENS + g * HOT
                        nc.scalar.copy(stage[:, :, bass.ds(at, HOT)].rearrange("p j t -> p t j"),
                                       bank(m, 6 + b).rearrange("p (t j) -> p t j", t=HOT)).then_inc(s["gate_out"], 1)
                        if (g + 1) % COLUMN_GROUPS == 0:
                            k = g // COLUMN_GROUPS
                            column(pair * 2 + k, k, pair, False, False)
                turns(act, i, body)

            act.wait_ge(s["ms_ready_c"], 1)
            nc.scalar.activation(root[:], ms[:], ACT.Sqrt).then_inc(s["root_ready_c"], 1)
            u_high(0, 0)
            u_high(1, 1)
            for i in range(NT):
                query_out(i)
                if i >= 1:
                    query_turned(i - 1)
            query_turned(NT - 1)
            score_out(0)
            for i in range(NT):
                ahead(act, i, alone)
                act.wait_ge(s["shifted"], i + 1)
                nc.scalar.activation(top[:], top[:], ACT.Exp).then_inc(s["exped"], 1)
                bridge(i, alone)
                act.wait_ge(s["picks_turned"], i + 1)
                nc.scalar.copy(picksT[:, i % 2].rearrange("p a t -> p (a t)"),
                               bank(m, 7)[:, 0:3 * P]).then_inc(s["picksT_ready"], 1)
                if i + 1 < NT:
                    score_out(i + 1)
                gates(i)
            tail(act, alone)

        @block.gpsimd
        def _(pool):
            def u_low(n, k, first):
                pool.wait_ge(s["u_high"], n + 1)
                if not first:
                    pool.wait_ge(s["hidden"], n - 1)
                nc.gpsimd.tensor_tensor(ul[:, k], u[:, k], uh[:, k].bitcast(F32), ALU.subtract).then_inc(s["u_low"], 1)

            def pair_of(pair, last):
                for k in range(2):
                    if not last:
                        u_low(pair * 2 + (k + 2), k, False)
            u_low(0, 0, True)
            u_low(1, 1, True)
            for i in range(NT):
                ahead(pool, i, lambda pair, first, last: pair_of(pair, last))
                bridge(i, lambda pair, first, last: pair_of(pair, last))
                turns(pool, i, lambda t, pair: pair_of(pair, False))
            tail(pool, lambda pair, first, last: pair_of(pair, last))

        @block.vector
        def _(dve):
            link = chain(dve, s["dve_order_c"])

            def normed(i):
                if i >= 2:
                    dve.wait_ge(s["hn_turned"], i - 1)
                nc.vector.tensor_scalar(hn[:, i % 2], m.stream[:, i, :], inv[:, i:i + 1], None,
                                        ALU.mult).then_inc(s["hn_ready"], 1)

            def normed_turned(i):
                dve.wait_ge(s["hn_turned"], i + 1)
                if i >= 2:
                    dve.wait_ge(s["queried"], i - 1)
                nc.vector.tensor_tensor(hnT[:, i % 2], bank(m, 0, 2).rearrange("p (c t) -> p c t", c=DC),
                                        bcast(m.ffn_gain[:], 2, P), ALU.mult).then_inc(s["hnT_ready"], 1)
                dve.wait_ge(s["hnT_ready"], i + 1)
                part = slice(i * P, (i + 1) * P)
                link(nc.vector.tensor_copy(m.xh[:, :, part], hnT[:, i % 2]))
                nc.vector.tensor_tensor(m.xl[:, :, part], hnT[:, i % 2], m.xh[:, :, part].bitcast(F32),
                                        ALU.subtract).then_inc(s["x_split"], 1)
                dve.wait_ge(s["x_split"], i + 1)

            def search(values, where, src, rows):
                def each(f):
                    for r in range(rows):
                        last = f(r)
                    return last
                link(each(lambda r: nc.vector.max(values[:, r, 0:8], src[:, r])))
                link(each(lambda r: nc.vector.max_index(where[:, r, 0:8], values[:, r, 0:8], src[:, r])))
                link(each(lambda r: nc.vector.match_replace(src[:, r], values[:, r, 0:8], src[:, r], TAKEN)))
                link(each(lambda r: nc.vector.max(values[:, r, 8:16], src[:, r])))
                return each(lambda r: nc.vector.max_index(where[:, r, 8:16], values[:, r, 8:16], src[:, r]))

            def pairs(out, part):
                first, second = part[:, 0:PEER_HEADS], part[:, PEER_HEADS:]
                at, a = 0, 0
                while a < PEER_TOPK:
                    n = ROWS[a][1]
                    k = sum(r[1] == n for r in ROWS)
                    dst = out[:, :, at:at + k * n].rearrange("p h (a b) -> p h a b", b=n)
                    last = nc.vector.tensor_tensor(dst, bcast(second[:, :, 0:n], 2, k), bcast(first[:, :, a:a + k], 3, n),
                                                   ALU.add)
                    at, a = at + k * n, a + k
                return last

            def chosen(i):
                dve.wait_ge(s["s_out"], i + 1)
                search(val, idx, s_sb, 2 * PEER_HEADS).then_inc(s["s_read"], 1)
                dve.wait_ge(s["s_read"], i + 1)
                link(nc.vector.tensor_copy(idx_f[:], idx[:]))
                rows = idx_f[:, 0:PEER_HEADS]
                link(nc.vector.tensor_scalar(rows, rows, float(N_KEYS), None, ALU.mult))
                link(pairs(cand, val[:]))
                link(pairs(code, idx_f[:]))
                link(search(top, top_at, cand, PEER_HEADS))
                link(nc.vector.tensor_copy(top_at_f[:], top_at[:]))
                link(nc.vector.tensor_copy(norm[:], top[:, :, 0]))
                nc.vector.tensor_tensor(top[:], top[:], bcast(norm[:], 2, PEER_TOPK), ALU.subtract).then_inc(s["shifted"], 1)
                for h in range(0, PEER_HEADS, HIT_HEADS):
                    some = slice(h, h + HIT_HEADS)
                    link(nc.vector.tensor_tensor(hits[:], bcast(top_at_f[:, some], 3, CANDS),
                                                 bcast(bcast(m.iota[:, 0:CANDS], 1, PEER_TOPK), 1, HIT_HEADS),
                                                 ALU.is_equal))
                    link(nc.vector.tensor_tensor(hits[:], hits[:], bcast(code[:, some], 2, PEER_TOPK), ALU.mult))
                    link(nc.vector.tensor_reduce(pick[:, some], hits[:], X, ALU.add))
                link(nc.vector.tensor_copy(pick_i[:, 2], pick[:].rearrange("p h k -> p (h k)")))
                nc.vector.tensor_scalar(pick_i[:, 0], pick_i[:, 2], 7, None, ALU.logical_shift_right)
                link(nc.vector.tensor_scalar(pick_i[:, 1], pick_i[:, 2], N_KEYS - 1, None, ALU.bitwise_and))
                if i >= 1:
                    dve.wait_ge(s["picks_turned"], i)
                nc.vector.tensor_copy(picks[:, 0:2], pick_i[:, 0:2])
                dve.wait_ge(s["exped"], i + 1)
                link(nc.vector.tensor_reduce(norm[:], top[:], X, ALU.add))
                link(nc.vector.reciprocal(norm[:], norm[:]))
                nc.vector.tensor_tensor(picks[:, 2].rearrange("p (h k) -> p h k", h=PEER_HEADS), top[:],
                                        bcast(norm[:], 2, PEER_TOPK), ALU.mult).then_inc(s["picks_ready"], 1)

            def one_hot(i):
                dve.wait_ge(s["picksT_ready"], i + 1)

                def body(t, pair):
                    for g in range(TURN_GROUPS):
                        b = g % 2
                        dve.wait_ge(s["hot_used"], t * TURN_GROUPS + (i * TURNS * TURN_GROUPS + g + 1))
                        for q in range(HOT):
                            tok = t * TURN_TOKENS + (g * HOT + q)
                            nc.vector.tensor_scalar(hot_i[:, b, q], m.iota[:], picksT[:, i % 2, 0, bass.ds(tok, 1)],
                                                    picksT[:, i % 2, 2, bass.ds(tok, 1)], ALU.is_equal, ALU.mult)
                            last_hot = nc.vector.tensor_scalar(hot_j[:, b, q], m.iota[:],
                                                               picksT[:, i % 2, 1, bass.ds(tok, 1)], None, ALU.is_equal)
                        last_hot.then_inc(s["hot_ready"], 1)
                turns(dve, i, body)

            nc.vector.tensor_scalar(ms[:], m.stream_sums[:], 1.0 / D, EPS, ALU.mult, ALU.add).then_inc(s["ms_ready_c"], 1)
            dve.wait_ge(s["root_ready_c"], 1)
            inverse_root(nc, link, inv[:], root[:], ms[:])
            normed(0)
            for i in range(NT):
                if i + 1 < NT:
                    normed(i + 1)
                normed_turned(i)
            for i in range(NT):
                chosen(i)
                one_hot(i)


RING = 4


def experts(nc, m, d):
    sb = placer(nc, m.free1)
    v = sb("v", [P, RING, D])
    vh = sb("vh", [P, RING, D], F32R)
    vl = sb("vl", [P, RING, D], F32R)
    gate = sb("gate", [P, RING, SEQ])
    act_w = sb("act_v", [P, RING, SEQ])
    wh = sb("wh", [P, RING, SEQ], F32R)
    wl = sb("wl", [P, RING, SEQ], F32R)

    loaded = [nc.alloc_semaphore(f"pair_loaded{k}") for k in range(RING // 2)]
    first_loaded = nc.alloc_semaphore("first_loaded")
    s = {n: nc.alloc_semaphore(n) for n in "v_high v_low gated w_high w_low summed added stored".split()}

    def rounds(engine, body):
        body(0, True, False)
        with engine.Fori(1, N_KEYS // RING - 1) as r:
            body(r, False, False)
        body(N_KEYS // RING - 1, False, True)

    with nc.Block() as block:
        @block.sync
        def _(sp):
            def body(r, first, last):
                for k in range(RING // 2):
                    n = r * RING + 2 * k
                    two = slice(2 * k, 2 * k + 2)
                    if not first:
                        sp.wait_ge(s["v_low"], n - RING + 2)
                        sp.wait_ge(s["w_low"], n - RING + 2)
                    if first and k == 0:
                        for j in range(2):
                            sp.dma_start(v[:, j], d.v[j]).then_inc(loaded[0] if j else first_loaded, 16)
                        for sem, count in m.route_stores:
                            sp.wait_ge(sem, count)
                        for j in range(2):
                            for dst, src in ((gate, d.gate_mat), (act_w, d.act_mat)):
                                sp.dma_start(dst[:, j], src[j]).then_inc(loaded[0] if j else first_loaded, 16)
                        continue
                    for dst, src in ((v, d.v), (gate, d.gate_mat), (act_w, d.act_mat)):
                        sp.dma_start(dst[:, two], src[bass.ds(n, 2)].rearrange("j i n -> i j n")
                                     ).then_inc(loaded[k], 16)
            rounds(sp, body)
            for i in range(NT):
                sp.wait_ge(s["added"], i + 1)
                sp.dma_start(d.out[i * P:(i + 1) * P, :], m.stream[:, i, :]).then_inc(s["stored"], 16)
            sp.wait_ge(s["stored"], 16 * NT)

        @block.tensor
        def _(pe):
            def body(r, first, last):
                for k in range(RING):
                    n = r * RING + k
                    pe.wait_ge(s["v_low"], n + 1)
                    pe.wait_ge(s["w_low"], n + 1)
                    for i in range(NT):
                        tok = slice(i * P, (i + 1) * P)
                        for p, (lhs, rhs) in enumerate(((wh, vh), (wh, vl), (wl, vh))):
                            for half in range(2):
                                mm = nc.tensor.matmul(bank(m, 2 * i + half), lhs[:, k, tok],
                                                      rhs[:, k, half * 512:(half + 1) * 512],
                                                      start=first and k == 0 and p == 0,
                                                      stop=last and k == RING - 1 and p == 2)
                    mm.then_inc(s["summed"], 1)
            rounds(pe, body)

        @block.scalar
        def _(act):
            def body(r, first, last):
                for k in range(RING):
                    n = r * RING + k
                    if first and k == 0:
                        act.wait_ge(first_loaded, 48)
                    elif k % 2 == 0 or first:
                        act.wait_ge(loaded[k // 2], r * 48 + 48)
                    if not first:
                        act.wait_ge(s["summed"], n - RING + 1)
                    nc.scalar.copy(vh[:, k], v[:, k]).then_inc(s["v_high"], 1)
                    act.wait_ge(s["gated"], n + 1)
                    nc.scalar.copy(wh[:, k], gate[:, k]).then_inc(s["w_high"], 1)
            rounds(act, body)

        @block.vector
        def _(dve):
            def body(r, first, last):
                for k in range(RING):
                    n = r * RING + k
                    if first and k == 0:
                        dve.wait_ge(first_loaded, 48)
                    elif k % 2 == 0 or first:
                        dve.wait_ge(loaded[k // 2], r * 48 + 48)
                    nc.vector.tensor_tensor(gate[:, k], gate[:, k], act_w[:, k], ALU.mult).then_inc(s["gated"], 1)
                    dve.wait_ge(s["v_high"], n + 1)
                    nc.vector.tensor_tensor(vl[:, k], v[:, k], vh[:, k].bitcast(F32), ALU.subtract
                                            ).then_inc(s["v_low"], 1)
                    dve.wait_ge(s["w_high"], n + 1)
                    nc.vector.tensor_tensor(wl[:, k], gate[:, k], wh[:, k].bitcast(F32), ALU.subtract
                                            ).then_inc(s["w_low"], 1)
            rounds(dve, body)
            dve.wait_ge(s["summed"], N_KEYS)
            for i in range(NT):
                nc.vector.tensor_tensor(m.stream[:, i, :], m.stream[:, i, :], bank(m, 2 * i, 2),
                                        ALU.add).then_inc(s["added"], 1)


class Dram:

    def __init__(self, t):
        self.x, self.meta_tokens = t["x"], t["meta_tokens"]
        self.w_wide, self.w_small = t["w_wide"], t["w_small"]
        self.mix_gain, self.ffn_gain = t["mix_gain"], t["ffn_gain"]
        self.cos, self.sin, self.icos, self.isin = t["cos"], t["sin"], t["icos"], t["isin"]
        self.a_q_norm_gain, self.a_k_norm_gain = t["a_q_norm_gain"], t["a_k_norm_gain"]
        self.b_q_norm_gain, self.b_k_norm_gain = t["b_q_norm_gain"], t["b_k_norm_gain"]
        self.a_subln_gain = t["a_subln_gain"]
        self.a_lambda_q1, self.a_lambda_k1 = t["a_lambda_q1"], t["a_lambda_k1"]
        self.a_lambda_q2, self.a_lambda_k2 = t["a_lambda_q2"], t["a_lambda_k2"]
        self.w_branch_a, self.w_branch_b, self.w_out = t["w_branch_a"], t["w_branch_b"], t["w_out"]
        self.w_query, self.sub_keys = t["w_query"], t["sub_keys"]
        self.u, self.v = t["u"], t["v"]
        self.gate_mat, self.act_mat = t["gate_mat"], t["act_mat"]
        self.out = t["out"]


def build(nc, args):
    d = Dram(args)
    m = Layer()
    place_shared(nc, m)
    project(nc, m, d)
    attend(nc, m, d)
    route(nc, m, d)
    experts(nc, m, d)


def rope_tables(np, dim):
    inv = (10000.0 ** (-np.arange(0, dim, 2) / dim)).astype(np.float32)
    ang = np.arange(KEYS, dtype=np.float32)[:, None] * inv[None, :]
    c, s = np.cos(ang.astype(np.float64)), np.sin(ang.astype(np.float64))
    out = []
    for t in (np.concatenate([c, c], 1), np.concatenate([-s, s], 1)):
        tiles = np.zeros((NT + 1, P, dim), np.float32)
        tiles[:NT] = t[META:].reshape(NT, P, dim)
        tiles[NT, :META] = t[:META]
        out.append(np.ascontiguousarray(tiles.transpose(1, 0, 2)))
    return out


def kernel(**inputs):
    import numpy as np
    import concourse.bacc as bacc
    from concourse.bass_utils import run_bass_kernel_spmd

    a = {k: np.asarray(v) for k, v in inputs.items()}

    def chunked(w):
        return np.ascontiguousarray(w.reshape(-1, P, w.shape[-1]).transpose(1, 0, 2))

    w_in = a["w_in"][0]
    names = ("aq", "ak", "av", "bq", "bk", "bv", "iq", "ik", "iw", "ga", "gb")
    widths = (512, 512, 512, 512, 64, 64, 512, 64, 8, 1024, 1024)
    cols, at = {}, 0
    for n, w in zip(names, widths):
        cols[n] = w_in[:, at:at + w]
        at += w
    wide = [cols["ak"], cols["av"], cols["aq"], cols["ga"][:, :512], cols["iq"], cols["ga"][:, 512:],
            cols["bq"], cols["gb"][:, :512], cols["gb"][:, 512:]]
    sub_keys = np.zeros((2, PEER_HALF, 2, PEER_HEADS, N_KEYS), np.float32)
    for c in range(2):
        sub_keys[c, :, c] = a["peer_sub_keys"][0, :, c].transpose(2, 0, 1)
    sub_keys = sub_keys.reshape(P, 2, PEER_HEADS, N_KEYS)
    cos, sin = rope_tables(np, HEAD)
    icos, isin = rope_tables(np, IDX_ROPE)
    arrays = {
        "x": np.ascontiguousarray(a["x"][0]),
        "meta_tokens": a["meta_tokens"],
        "w_wide": np.stack([chunked(w) for w in wide]),
        "w_small": chunked(np.concatenate([cols[n] for n in ("bk", "bv", "ik", "iw")], 1)),
        "mix_gain": np.ascontiguousarray(a["mix_norm_gain"][0].reshape(DC, P).T),
        "ffn_gain": np.ascontiguousarray(a["ffn_norm_gain"][0].reshape(DC, P).T),
        "cos": cos, "sin": sin, "icos": icos, "isin": isin,
        "w_branch_a": chunked(a["w_branch_a"][0]),
        "w_branch_b": chunked(a["w_branch_b"][0]),
        "w_out": chunked(a["w_out"][0]),
        "w_query": chunked(a["peer_w_query"][0]),
        "sub_keys": sub_keys,
        "u": np.ascontiguousarray(a["peer_u"][0].reshape(N_KEYS, N_KEYS, DC, P).transpose(1, 3, 2, 0)),
        "v": np.ascontiguousarray(a["peer_v"][0].reshape(N_KEYS, N_KEYS, D).transpose(1, 0, 2)),
    }
    for n in ("a_q_norm_gain", "a_k_norm_gain", "b_q_norm_gain", "b_k_norm_gain", "a_subln_gain",
              "a_lambda_q1", "a_lambda_k1", "a_lambda_q2", "a_lambda_k2"):
        arrays[n] = a[n][0]

    nc = bacc.Bacc("TRN2", target_bir_lowering=False, num_devices=1)
    args = {n: nc.dram_tensor("in_" + n, v.shape, mybir.dt.from_np(v.dtype), kind="ExternalInput").ap()
            for n, v in arrays.items()}
    args["out"] = nc.dram_tensor("out", (SEQ, D), F32, kind="ExternalOutput").ap()
    for n in ("gate_mat", "act_mat"):
        args[n] = nc.dram_tensor(n, (N_KEYS, N_KEYS, SEQ), F32, kind="Internal").ap()
    build(nc, args)
    r = run_bass_kernel_spmd(nc, [{"in_" + n: v for n, v in arrays.items()}], core_ids=[0])
    return r.results[0]["out"].reshape(1, SEQ, D)
```
